# Optimizing a Trainium2 kernel written in Bass

```python
import jax
import jax.numpy as jnp
from jax import lax
import numpy as np

'''One inference step of a hybrid decoder layer with parallel head groups.

Per layer: RMSNorm -> one combined input projection whose columns are split between
  (A) DSA-style sparse attention: a light token indexer scores every causal key,
      each query keeps top-k = min(256, L//4) keys and attends to the GATHERED K/V
      (GQA, partial rotary theta=500000 on the first quarter of each head dim), and
  (B) RetNet multi-scale retention in chunkwise-recurrent form (per-head decay
      gamma_h = 1 - 2^(-5-h), own full rotary theta=10000), per-head group norm and swish gate;
-> head-group outputs concatenated -> one output projection -> residual;
RMSNorm -> PEER product-key single-neuron expert retrieval FFN -> residual; final RMSNorm.

Inputs:
  x_prompt (BATCH, SEQ, D_MODEL), x_sample (DEC_BATCH, DEC_SEQ, D_MODEL)
  cache_k, cache_v   (DEPTH, N_PHYS, PAGE_SIZE, KV_HEADS, ATT_HEAD_DIM)   paged, rotated keys
  cache_idx_k        (DEPTH, N_PHYS, PAGE_SIZE, IDX_DIM)                  paged indexer keys
  state_ret          (DEPTH, DEC_BATCH, RET_HEADS, RET_HEAD_DIM, RET_HEAD_DIM)
  page_table         (DEC_BATCH, N_PAGES) int32, N_PAGES = PAST_LEN // PAGE_SIZE
  weights stacked over a leading DEPTH axis (final_norm_w is (D_MODEL,)).
Returns the tuple
  (y_prompt (BATCH, SEQ, D_MODEL), y_sample (DEC_BATCH, DEC_SEQ, D_MODEL),
   k_prompt (DEPTH, BATCH, SEQ, KV_HEADS, ATT_HEAD_DIM), v_prompt (same),
   idx_k_prompt (DEPTH, BATCH, SEQ, IDX_DIM), ret_state_prompt (DEPTH, BATCH, RET_HEADS, RET_HEAD_DIM, RET_HEAD_DIM),
   k_sample (DEPTH, DEC_BATCH, DEC_SEQ, KV_HEADS, ATT_HEAD_DIM), v_sample (same),
   idx_k_sample (DEPTH, DEC_BATCH, DEC_SEQ, IDX_DIM), ret_state_sample (DEPTH, DEC_BATCH, RET_HEADS, RET_HEAD_DIM, RET_HEAD_DIM)).
'''

D_MODEL = 1024
BATCH = 1
SEQ = 1024
DEPTH = 1
DEC_BATCH = 8
DEC_SEQ = 4
PAST_LEN = 2048
PAGE_SIZE = 128

ATT_HEADS = 8
ATT_HEAD_DIM = 64
KV_HEADS = 2
ATT_GROUP = ATT_HEADS // KV_HEADS
ATT_WIDTH = ATT_HEADS * ATT_HEAD_DIM
ROPE_THETA = 500000.0
ATT_ROPE_DIMS = ATT_HEAD_DIM // 4
IDX_HEADS = 8
IDX_DIM = 64
IDX_ROPE_DIMS = IDX_DIM // 4
TOPK_MAX = 256
Q_BLOCK = 128
RET_HEADS = 4
RET_HEAD_DIM = 128
RET_WIDTH = RET_HEADS * RET_HEAD_DIM
RET_ROPE_THETA = 10000.0
RET_CHUNK = 128
MIX_WIDTH = ATT_WIDTH + RET_WIDTH
PEER_HEADS = 8
PEER_NKEYS = 128
PEER_EXPERTS = PEER_NKEYS * PEER_NKEYS
PEER_KEY_DIM = 128
PEER_HALF = PEER_KEY_DIM // 2
PEER_TOPK = 16
PEER_BLOCK = 128
NORM_EPS = 1e-6
GN_EPS = 1e-6
IN_SPLITS = (ATT_WIDTH, KV_HEADS * ATT_HEAD_DIM, KV_HEADS * ATT_HEAD_DIM,
             IDX_HEADS * IDX_DIM, IDX_DIM, IDX_HEADS,
             RET_WIDTH, RET_WIDTH, RET_WIDTH, RET_WIDTH)
IN_WIDTH = sum(IN_SPLITS)

kernel_name = 'hymba_dsa_retnet_peer_step'

F32 = jnp.float32

def rms_norm(x, w):
    xf = x.astype(F32)
    y = xf * lax.rsqrt(jnp.mean(xf * xf, axis=-1, keepdims=True) + NORM_EPS)
    return (y * w.astype(F32)).astype(x.dtype)

def rope(x, pos, rot_dims, theta):
    half = rot_dims // 2
    inv = 1.0 / (theta ** (jnp.arange(half, dtype=F32) / half))
    ang = pos.astype(F32)[:, None] * inv[None, :]
    cos = jnp.cos(ang)[:, None, :]
    sin = jnp.sin(ang)[:, None, :]
    xr = x[..., :rot_dims].astype(F32)
    x1, x2 = xr[..., :half], xr[..., half:]
    rot = jnp.concatenate([x1 * cos - x2 * sin, x2 * cos + x1 * sin], axis=-1).astype(x.dtype)
    return jnp.concatenate([rot, x[..., rot_dims:]], axis=-1)

def split_cols(h):
    outs = []
    off = 0
    for n in IN_SPLITS:
        outs.append(h[..., off:off + n])
        off += n
    return outs

def mixer_inputs(xn, pos, w_in_l):
    B, T, _ = xn.shape
    qa, ka, va, qi, ki, wi, qr, kr, vr, gr = split_cols(xn @ w_in_l)
    qa = rope(qa.reshape(B, T, ATT_HEADS, ATT_HEAD_DIM), pos, ATT_ROPE_DIMS, ROPE_THETA)
    ka = rope(ka.reshape(B, T, KV_HEADS, ATT_HEAD_DIM), pos, ATT_ROPE_DIMS, ROPE_THETA)
    va = va.reshape(B, T, KV_HEADS, ATT_HEAD_DIM)
    qi = rope(qi.reshape(B, T, IDX_HEADS, IDX_DIM), pos, IDX_ROPE_DIMS, ROPE_THETA)
    ki = rope(ki.reshape(B, T, 1, IDX_DIM), pos, IDX_ROPE_DIMS, ROPE_THETA)[:, :, 0]
    wi = wi * (IDX_HEADS ** -0.5)
    qr = rope(qr.reshape(B, T, RET_HEADS, RET_HEAD_DIM), pos, RET_HEAD_DIM, RET_ROPE_THETA)
    kr = rope(kr.reshape(B, T, RET_HEADS, RET_HEAD_DIM), pos, RET_HEAD_DIM, RET_ROPE_THETA) * (RET_HEAD_DIM ** -0.5)
    vr = vr.reshape(B, T, RET_HEADS, RET_HEAD_DIM)
    return qa, ka, va, qi, ki, wi, qr, kr, vr, gr

def indexer_scores(qi, wi, ki):
    dots = jnp.einsum('bthd,bld->bthl', qi, ki).astype(F32) * (IDX_DIM ** -0.5)
    return jnp.einsum('bth,bthl->btl', wi.astype(F32), jax.nn.relu(dots))

def sparse_attend(q, k_sel, v_sel, valid):
    B, T = q.shape[:2]
    qg = q.reshape(B, T, KV_HEADS, ATT_GROUP, ATT_HEAD_DIM)
    logits = jnp.einsum('btcgd,btscd->btcgs', qg, k_sel).astype(F32) * (ATT_HEAD_DIM ** -0.5)
    logits = jnp.where(valid[:, :, None, None, :], logits, -jnp.inf)
    p = jax.nn.softmax(logits, axis=-1)
    o = jnp.einsum('btcgs,btscd->btcgd', p.astype(v_sel.dtype), v_sel)
    return o.reshape(B, T, ATT_WIDTH)

def prompt_dsa(qa, ka, va, qi, ki, wi):
    B, S = qa.shape[:2]
    topk = min(TOPK_MAX, S // 4)
    n_blocks = S // Q_BLOCK
    bidx = jnp.arange(B)[:, None, None]
    key_pos = jnp.arange(S)

    def block(i):
        t0 = i * Q_BLOCK
        q_b = lax.dynamic_slice_in_dim(qa, t0, Q_BLOCK, axis=1)
        qi_b = lax.dynamic_slice_in_dim(qi, t0, Q_BLOCK, axis=1)
        wi_b = lax.dynamic_slice_in_dim(wi, t0, Q_BLOCK, axis=1)
        qpos = t0 + jnp.arange(Q_BLOCK)
        sc = indexer_scores(qi_b, wi_b, ki)
        sc = jnp.where((key_pos[None, :] <= qpos[:, None])[None], sc, -jnp.inf)
        _, sel = lax.top_k(sc, topk)
        valid = sel <= qpos[None, :, None]
        return sparse_attend(q_b, ka[bidx, sel], va[bidx, sel], valid)

    out = lax.map(block, jnp.arange(n_blocks))
    return out.transpose(1, 0, 2, 3).reshape(B, S, ATT_WIDTH)

def sample_dsa(qa, ka, va, qi, ki, wi, cache_k_l, cache_v_l, cache_idx_k_l, page_table):
    Bd, T = qa.shape[:2]
    past_len = page_table.shape[1] * PAGE_SIZE
    L = past_len + T
    topk = min(TOPK_MAX, L // 4)
    bidx = jnp.arange(Bd)[:, None, None]
    past_ik = cache_idx_k_l[page_table].reshape(Bd, past_len, IDX_DIM)
    all_ik = jnp.concatenate([past_ik, ki.astype(past_ik.dtype)], axis=1)
    sc = indexer_scores(qi, wi, all_ik)
    key_pos = jnp.arange(L)
    qpos = past_len + jnp.arange(T)
    sc = jnp.where((key_pos[None, :] <= qpos[:, None])[None], sc, -jnp.inf)
    _, sel = lax.top_k(sc, topk)
    valid = sel <= qpos[None, :, None]
    in_past = sel < past_len
    ps = jnp.minimum(sel, past_len - 1)
    phys = page_table[bidx, ps // PAGE_SIZE]
    off = ps % PAGE_SIZE
    nidx = jnp.clip(sel - past_len, 0, T - 1)
    k_sel = jnp.where(in_past[..., None, None], cache_k_l[phys, off], ka[bidx, nidx].astype(cache_k_l.dtype))
    v_sel = jnp.where(in_past[..., None, None], cache_v_l[phys, off], va[bidx, nidx].astype(cache_v_l.dtype))
    return sparse_attend(qa, k_sel.astype(qa.dtype), v_sel.astype(qa.dtype), valid)

def ret_log_decay():
    return jnp.log1p(-(2.0 ** (-5.0 - jnp.arange(RET_HEADS, dtype=F32))))

def retention_chunk(state, q, k, v):
    C = q.shape[1]
    lg = ret_log_decay()
    i = jnp.arange(C, dtype=F32)
    diff = i[:, None] - i[None, :]
    dmask = jnp.where(diff >= 0, jnp.exp(lg[:, None, None] * jnp.maximum(diff, 0.0)), 0.0)
    q_dec = jnp.exp(lg[None, :] * (i[:, None] + 1.0))
    k_dec = jnp.exp(lg[None, :] * (C - 1.0 - i[:, None]))
    chunk_dec = jnp.exp(lg * C)
    qf, kf, vf = q.astype(F32), k.astype(F32), v.astype(F32)
    att = jnp.einsum('bihd,bjhd->bhij', qf, kf) * dmask[None]
    o = (jnp.einsum('bhij,bjhe->bihe', att, vf)
         + jnp.einsum('bihd,bhde->bihe', qf, state) * q_dec[None, :, :, None])
    new_state = (state * chunk_dec[None, :, None, None]
                 + jnp.einsum('bjhd,bjhe->bhde', kf * k_dec[None, :, :, None], vf))
    return new_state, o

def prompt_retention(q, k, v):
    B, S, H, D = q.shape
    nc = S // RET_CHUNK

    def resh(a):
        return a.reshape(B, nc, RET_CHUNK, H, D).swapaxes(0, 1)

    s0 = jnp.zeros((B, H, D, D), F32)
    s_fin, o = lax.scan(lambda s, xs: retention_chunk(s, xs[0], xs[1], xs[2]), s0, (resh(q), resh(k), resh(v)))
    return o.swapaxes(0, 1).reshape(B, S, H, D), s_fin

def retention_out(o, g, gn_w_l):
    B, T = o.shape[:2]
    mu = jnp.mean(o, axis=-1, keepdims=True)
    var = jnp.mean(jnp.square(o - mu), axis=-1, keepdims=True)
    on = ((o - mu) * lax.rsqrt(var + GN_EPS)).reshape(B, T, RET_WIDTH) * gn_w_l.astype(F32)
    return (jax.nn.silu(g.astype(F32)) * on).astype(g.dtype)

def peer_ffn(x, w_q, sub_keys_1, sub_keys_2, u_emb, v_emb):
    N = x.shape[0]
    nb = -(-N // PEER_BLOCK)
    xp = jnp.pad(x, ((0, nb * PEER_BLOCK - N), (0, 0)))

    def block(xb):
        q = (xb @ w_q).reshape(PEER_BLOCK, PEER_HEADS, 2, PEER_HALF)
        s1 = jnp.einsum('thd,kd->thk', q[:, :, 0], sub_keys_1).astype(F32)
        s2 = jnp.einsum('thd,kd->thk', q[:, :, 1], sub_keys_2).astype(F32)
        v1, i1 = lax.top_k(s1, PEER_TOPK)
        v2, i2 = lax.top_k(s2, PEER_TOPK)
        cand = (v1[..., :, None] + v2[..., None, :]).reshape(PEER_BLOCK, PEER_HEADS, PEER_TOPK * PEER_TOPK)
        cid = (i1[..., :, None] * PEER_NKEYS + i2[..., None, :]).reshape(PEER_BLOCK, PEER_HEADS, PEER_TOPK * PEER_TOPK)
        sv, si = lax.top_k(cand, PEER_TOPK)
        eid = jnp.take_along_axis(cid, si, axis=-1)
        gate = jax.nn.softmax(sv, axis=-1)
        hval = jnp.einsum('thkd,td->thk', u_emb[eid], xb).astype(F32)
        coef = (gate * jax.nn.gelu(hval, approximate=False)).astype(xb.dtype)
        return jnp.einsum('thk,thkd->td', coef, v_emb[eid])

    y = lax.map(block, xp.reshape(nb, PEER_BLOCK, x.shape[1]))
    return y.reshape(nb * PEER_BLOCK, x.shape[1])[:N]

def ffn_residual(h, norm_w_l, w_q, sk1, sk2, u_emb, v_emb):
    B, T, D = h.shape
    y = peer_ffn(rms_norm(h, norm_w_l).reshape(B * T, D), w_q, sk1, sk2, u_emb, v_emb)
    return h + y.reshape(B, T, D).astype(h.dtype)

def setup_inputs(seed: int = 0) -> dict:
    key = jax.random.key(seed)
    ks = jax.random.split(key, 20)
    n_pages = PAST_LEN // PAGE_SIZE
    n_used = DEC_BATCH * n_pages
    n_phys = n_used + (n_used + 3) // 4
    perm = jax.random.permutation(ks[0], n_phys)[:n_used]
    page_table = perm.reshape(DEC_BATCH, n_pages).astype(jnp.int32)
    nrm = jax.random.normal
    return {
        'x_prompt': nrm(ks[1], (BATCH, SEQ, D_MODEL), F32),
        'x_sample': nrm(ks[2], (DEC_BATCH, DEC_SEQ, D_MODEL), F32),
        'cache_k': nrm(ks[3], (DEPTH, n_phys, PAGE_SIZE, KV_HEADS, ATT_HEAD_DIM), F32),
        'cache_v': nrm(ks[4], (DEPTH, n_phys, PAGE_SIZE, KV_HEADS, ATT_HEAD_DIM), F32),
        'cache_idx_k': nrm(ks[5], (DEPTH, n_phys, PAGE_SIZE, IDX_DIM), F32),
        'state_ret': nrm(ks[6], (DEPTH, DEC_BATCH, RET_HEADS, RET_HEAD_DIM, RET_HEAD_DIM), F32),
        'page_table': page_table,
        'norm_attn_w': 1.0 + 0.02 * nrm(ks[7], (DEPTH, D_MODEL), F32),
        'w_in': nrm(ks[8], (DEPTH, D_MODEL, IN_WIDTH), F32) * D_MODEL ** -0.5,
        'ret_gn_w': 1.0 + 0.02 * nrm(ks[9], (DEPTH, RET_WIDTH), F32),
        'w_out': nrm(ks[10], (DEPTH, MIX_WIDTH, D_MODEL), F32) * MIX_WIDTH ** -0.5,
        'norm_ffn_w': 1.0 + 0.02 * nrm(ks[11], (DEPTH, D_MODEL), F32),
        'peer_w_q': nrm(ks[12], (DEPTH, D_MODEL, PEER_HEADS * PEER_KEY_DIM), F32) * D_MODEL ** -0.5,
        'peer_sub_keys_1': nrm(ks[13], (DEPTH, PEER_NKEYS, PEER_HALF), F32) * PEER_HALF ** -0.5,
        'peer_sub_keys_2': nrm(ks[14], (DEPTH, PEER_NKEYS, PEER_HALF), F32) * PEER_HALF ** -0.5,
        'peer_u': nrm(ks[15], (DEPTH, PEER_EXPERTS, D_MODEL), F32) * D_MODEL ** -0.5,
        'peer_v': nrm(ks[16], (DEPTH, PEER_EXPERTS, D_MODEL), F32) * PEER_HEADS ** -0.5,
        'final_norm_w': 1.0 + 0.02 * nrm(ks[17], (D_MODEL,), F32),
    }

def reference(x_prompt, x_sample, cache_k, cache_v, cache_idx_k, state_ret, page_table,
              norm_attn_w, w_in, ret_gn_w, w_out, norm_ffn_w, peer_w_q,
              peer_sub_keys_1, peer_sub_keys_2, peer_u, peer_v, final_norm_w):
    hp = x_prompt
    hs = x_sample
    S = x_prompt.shape[1]
    T = x_sample.shape[1]
    pos_p = jnp.arange(S)
    pos_s = page_table.shape[1] * PAGE_SIZE + jnp.arange(T)
    kp_l, vp_l, ikp_l, sp_l = [], [], [], []
    ks_l, vs_l, iks_l, ss_l = [], [], [], []
    for l in range(DEPTH):
        qa, ka, va, qi, ki, wi, qr, kr, vr, gr = mixer_inputs(rms_norm(hp, norm_attn_w[l]), pos_p, w_in[l])
        att = prompt_dsa(qa, ka, va, qi, ki, wi)
        o_r, s_r = prompt_retention(qr, kr, vr)
        mix = jnp.concatenate([att, retention_out(o_r, gr, ret_gn_w[l])], axis=-1)
        hp = hp + mix @ w_out[l]
        hp = ffn_residual(hp, norm_ffn_w[l], peer_w_q[l], peer_sub_keys_1[l], peer_sub_keys_2[l], peer_u[l], peer_v[l])
        kp_l.append(ka)
        vp_l.append(va)
        ikp_l.append(ki)
        sp_l.append(s_r.astype(x_prompt.dtype))
        qa, ka, va, qi, ki, wi, qr, kr, vr, gr = mixer_inputs(rms_norm(hs, norm_attn_w[l]), pos_s, w_in[l])
        att = sample_dsa(qa, ka, va, qi, ki, wi, cache_k[l], cache_v[l], cache_idx_k[l], page_table)
        s_new, o_r = retention_chunk(state_ret[l].astype(F32), qr, kr, vr)
        mix = jnp.concatenate([att, retention_out(o_r, gr, ret_gn_w[l])], axis=-1)
        hs = hs + mix @ w_out[l]
        hs = ffn_residual(hs, norm_ffn_w[l], peer_w_q[l], peer_sub_keys_1[l], peer_sub_keys_2[l], peer_u[l], peer_v[l])
        ks_l.append(ka)
        vs_l.append(va)
        iks_l.append(ki)
        ss_l.append(s_new.astype(state_ret.dtype))
    y_prompt = rms_norm(hp, final_norm_w)
    y_sample = rms_norm(hs, final_norm_w)
    return (y_prompt, y_sample,
            jnp.stack(kp_l), jnp.stack(vp_l), jnp.stack(ikp_l), jnp.stack(sp_l),
            jnp.stack(ks_l), jnp.stack(vs_l), jnp.stack(iks_l), jnp.stack(ss_l))


_drawn_inputs = setup_inputs


def setup_inputs(seed=0):
    import zlib

    import numpy as np

    out = dict(_drawn_inputs(seed))
    spreads = {}
    factors = {'ret_gn_w': 8.938, 'final_norm_w': 23.421, 'norm_ffn_w': 10.518, 'cache_k': 2.831}
    for name, (base, spread) in spreads.items():
        noise = np.random.default_rng([zlib.crc32(name.encode()), seed]).standard_normal(out[name].shape)
        drawn = base * np.exp(spread * noise) if base else spread * noise
        out[name] = jnp.asarray(drawn.astype(out[name].dtype))
    for name, factor in factors.items():
        out[name] = (out[name] * factor).astype(out[name].dtype)
    return out
```

```python
from contextlib import ExitStack

import numpy as np

import concourse.bass as bass
from concourse import mybir

F32 = mybir.dt.float32
I32 = mybir.dt.int32
U32 = mybir.dt.uint32
ALU = mybir.AluOpType
ACT = mybir.ActivationFunctionType
AX = mybir.AxisListType

P = 128
D = 1024
KC = D // P
SEQ = 1024
NB, NT = 8, 4
NS = NB * NT
PAST = 2048
PAGE = 128
TILES = SEQ // P
SAMPLE = TILES
HA, HD, KVH = 8, 64, 2
HI = 8
HR, RD = 4, 128
QA, KA, VA, QI, KI, WI, QR, KR, VR, GR = 0, 512, 640, 768, 1280, 1344, 1352, 1864, 2376, 2888
INW = 3400
TOPK = 256
ROUNDS = TOPK // 8
PH, PK, NKEY, EXPERTS = 8, 16, 128, 128 * 128
SLOTS = PH * PK
RING = 8
BATCH = 4
EPS = 1e-6
BIG = 1.0e30
OUTSIDE = -3.0e38
CHOSEN = -3.4e38
BLK = 16
SL = PAST + NS
LOGG = [float(np.log1p(-(2.0 ** (-5.0 - h)))) for h in range(HR)]


def constants():
    f = np.float32
    pos = np.concatenate([np.arange(SEQ), PAST + np.tile(np.arange(NT), NB)]).astype(f)

    def table(half, theta):
        ang = pos[:, None] * (f(1.0) / (f(theta) ** (np.arange(half, dtype=f) / f(half)))).astype(f)[None, :]
        return np.cos(ang), np.sin(ang)

    ca, sa = table(8, 500000.0)
    cr, sr = table(64, 10000.0)
    rope = np.concatenate([ca, sa, cr, sr], 1).astype(f)

    def decay(n, same):
        i = np.arange(n)
        lg = np.array(LOGG)
        c = NT if same else n
        within = i % c
        diff = within[None, :] - within[:, None]
        ok = (diff >= 0) & ((i[:, None] // c) == (i[None, :] // c))
        mask = np.where(ok[:, None, :], np.exp(lg[None, :, None] * np.maximum(diff, 0)[:, None, :]), 0) * RD ** -0.5
        qd = np.broadcast_to(np.exp(lg[:, None] * (within[None, :] + 1))[None], (P, HR, n))
        kd = np.exp(lg[None, :] * (c - 1 - within[:, None])) * RD ** -0.5
        return mask.astype(f), qd.astype(f), kd.astype(f)

    md, qd, kd = decay(P, False)
    ms, qs, ks = decay(NS, True)
    main = np.zeros((P, 128 + 16 + 128 + 4 + 128), f)
    main[:, 0:128] = np.eye(P)
    main[:, 128:144] = np.arange(16)
    main[:, 144:272] = np.where(np.arange(P)[None, :] <= np.arange(P)[:, None], 0, OUTSIDE)
    main[:, 272:276] = kd
    main[:, 276] = np.arange(P) % 8
    dec = np.concatenate([md.reshape(P, -1), qd.reshape(P, -1)], 1)
    tok = np.arange(NS)
    s32 = np.zeros((NS, 128 + 4 + 8 + NB * NS + NS), f)
    s32[:, 0:128] = ms.reshape(NS, -1)
    s32[:, 128:132] = ks
    s32[:, 132:140] = (tok[:, None] // NT) == np.arange(NB)[None, :]
    rep = np.zeros((NS, NB, HA, NT), f)
    for k in range(NS):
        rep[k, k // NT, :, k % NT] = 1
    s32[:, 140:140 + NB * NS] = rep.reshape(NS, -1)
    same = (tok[:, None] // NT == tok[None, :] // NT) & (tok[None, :] <= tok[:, None])
    s32[:, 396:428] = np.where(same, 0, OUTSIDE)
    s128 = np.zeros((P, 128 + NB * NS + 128), f)
    s128[:, 0:128] = qs.reshape(P, -1)
    s128[:, 128:384] = np.broadcast_to(np.eye(NB)[:, :, None], (NB, NB, NT)).reshape(1, -1)
    rows = np.arange(P) % NS // NT
    s128[:, 384:512] = (rows[:, None] // (HA // KVH)) == (np.arange(P)[None, :] // HD)
    return rope, main, dec, s32, s128


def psum_plan(schedule):
    names = []
    for what, t in schedule:
        if what == "project":
            if t == 0:
                names += [("xT", t, g) for g in range(2)]
            if t < SAMPLE:
                names += [("xT", t + 1, g) for g in range(2)]
            names += [("proj", t, n) for n in range(7)]
            if t:
                names.append(("keysT", t - 1))
            if t == SAMPLE:
                names.append(("keysT", t))
        elif what == "heads":
            names += [(w, t) for w in ("qiT", "qaT", "qrT", "krT", "decayed", "state")]
        elif what == "scores":
            names += [("score", t, c, h) for c in range((t + 4) // 4) for h in range(HI)]
        elif what == "attend":
            nch = (t + 4) // 4
            for h in range(HA + 1):
                if h < HA:
                    names += [("logit", t, h, c) for c in range(nch)]
                if h:
                    names += [("pT", t, h - 1, c) for c in range(nch)]
        elif what == "sheads":
            names += [(w, t) for w in ("qiT", "qaT", "qrT", "krT", "decayed", "wiT")] + [("sstate", b) for b in range(NB)]
        elif what == "sscores":
            for b in range(NB):
                names += [(w, b, c) for c in range(5) for w in (("skT", "sdot", "ssum") if c < 4 else ("sdot", "ssum"))]
        elif what == "sattend":
            for g in range(2):
                for b in range(4 * g, 4 * g + 4):
                    names += [(w, b, c) for c in range(5) for w in (("sKT", "slog") if c < 4 else ("slog",))]
                names += [("spT", g, c) for c in range(5)]
            names += []
        elif what == "output":
            names += [("mixT", t, 0), ("mixT", t, 1), ("out", t, 0), ("out", t, 1), ("nT", t, 0), ("nT", t, 1),
                      ("peerq", t, 0), ("peerq", t, 1)] + [("keys", t, n) for n in range(4)]
    return {name: (k % 4, k // 4) for k, name in enumerate(names)}


def long_plan(schedule):
    names = []
    for what, t in schedule:
        if what == "heads":
            names.append(("ret", t))
        elif what == "sheads":
            names.append(("ret", t))
        elif what == "attend":
            names.append(("att", t))
        elif what == "sattend":
            names += [("satt", g) for g in range(2)]
    return {name: (k % 2, k // 2) for k, name in enumerate(names)}


def make_schedule():
    s = [("project", t) for t in range(TILES + 1)]
    s += [("heads", 0), ("mask", 0), ("attend", 0), ("output", 0), ("choose", 0)]
    for t in range(TILES + 1):
        n = t + 1
        if n < TILES:
            steps = [[("heads", n)]]
            steps += [[("scores", n)], [("topk", 4 * n)], [("topk", 4 * n + 1)], [("topk", 4 * n + 2)], [("topk", 4 * n + 3), ("mask", n)]] if n >= 2 else [[("mask", n)]]
            steps += [[("attend", n)], [("output", n)], [("choose", n)]]
        elif n == SAMPLE:
            steps = [[("sheads", n)], [("sscores", n)]] + [[("topk", 4 * n + k)] for k in range(4)]
            steps += [[("mask", n), ("sattend", n)], [("output", n)], [("choose", n)]]
        else:
            steps = []
        heads = [[("peer", 8 * t + h)] for h in range(PH)]
        s.append(("seed", t))
        while heads or steps:
            if heads:
                s += heads.pop(0)
            take = max(1, -(-len(steps) // (len(heads) + 1))) if steps else 0
            for _ in range(take):
                s += steps.pop(0)
        s.append(("finish", t))
    return s


def build(nc, x_p, x_s, cache_k, cache_v, cache_ik, state_in, pages, w_in, w_out, w_q, sk, uv,
          cols, wffn, wfin, c_rope, c_main, c_dec, c_s32, c_s128,
          y_p, y_s, k_p, v_p, ik_p, st_p, k_s, v_s, ik_s, st_s):
    schedule = make_schedule()
    short, long = psum_plan(schedule), long_plan(schedule)
    score_no = {n[1:]: k for k, n in enumerate(n for n in short if n[0] == "score")}
    turned_no = {n[1:]: k for k, n in enumerate(n for n in short if n[0] == "pT")}

    norm_no = {e: k + 1 for k, e in enumerate(e for e in schedule if e[0] in ("output", "finish"))}

    def rows(t):
        return P if t < TILES else NS

    def x_of(t):
        return x_p[t * P:(t + 1) * P, :] if t < TILES else x_s

    with ExitStack() as ctx:
        def sb(name, shape, dt=F32):
            return ctx.enter_context(nc.sbuf_tensor(name, shape, dt))

        def sem(name):
            return ctx.enter_context(nc.semaphore(name))

        h_dram = nc.dram_tensor("h_scratch", (SEQ + NS, INW), F32, kind="Internal").ap()
        a_dram = nc.dram_tensor("a_scratch", (NB * HA * NT, HD), F32, kind="Internal").ap()

        weights = sb("weights", [P, 128 * 256])
        main = sb("main", [P, 404])
        dec = sb("dec", [P, 1024])
        nw = sb("nw", [P, D])
        keysT = sb("keysT", [P, 256])
        state = sb("state", [P, HR, RD])
        kv = sb("kv", [P, 2048 + SL])
        Hb = sb("Hb", [P, INW])
        spare = sb("spare", [P, 2048 + SL])
        mid = sb("mid", [P, 2, 512])
        h1 = sb("h1", [P, D])
        xn = sb("xn", [P, 2, D])
        eid = sb("eid", [P, 2, SLOTS], I32)
        gate = sb("gate", [P, 2, PH, PK])
        idx8 = sb("idx8", [P, 2, 8], I32)
        diag = sb("diag", [P, 4, P])
        colw = sb("colw", [P, 12])
        tiny = sb("tiny", [P, 64])
        nmx = sb("nmx", [P, 8])
        rs = sb("rs", [P, 8])
        tinya = sb("tinya", [P, 4])
        tinyb = sb("tinyb", [P, 4])
        hv = sb("hv", [P, 8])
        gl = sb("gl", [P, 8])
        coef = sb("coef", [P, 8])

        win = weights[:, 0:KC * INW].rearrange("p (k n) -> p k n", k=KC)
        xa = [weights[:, 27264 + 1024 * i:27264 + 1024 * (i + 1)] for i in range(2)]
        xT = [weights[:, 29312:30336].rearrange("p (k n) -> p k n", k=KC),
              mid[:].rearrange("p a n -> p (a n)").rearrange("p (k n) -> p k n", k=KC)]
        rot = [weights[:, 30336 + 144 * i:30336 + 144 * (i + 1)] for i in range(2)]
        rt = weights[:, 30624:30624 + 2048].rearrange("p (a n) -> p a n", a=4)
        wout_sb = weights[:, 0:8192].rearrange("p (k n) -> p k n", k=KC)
        wq_sb = weights[:, 8192:16384].rearrange("p (k n) -> p k n", k=KC)
        ring = weights[:, 16384:32768].rearrange("p (s n) -> p s n", s=RING)
        ident = main[:, 0:128]
        iota16 = main[:, 128:144]
        causal = main[:, 144:272]
        kT = kv[:, 0:1024]
        kiT = kv[:, 1024:2048]
        vall = kv[:, 2048:3072].rearrange("p (t n) -> p t n", t=TILES)
        sc = kv[:, 3072:4096]
        states = kv[:, 0:NB * 512].rearrange("p (b h e) -> p b h e", b=NB, h=HR)
        G = kv[:, 0:2048]
        scs = kv[0:NS, 2048:2048 + SL]
        qiT, qaT, qrT, krT = (spare[:, 512 * k:512 * (k + 1)].rearrange("p (g n) -> p g n", g=4) for k in range(4))
        H = [Hb, spare[:, 0:INW]]
        S = spare[:, 2048:2048 + SL]
        v16 = spare[:, 1024:1280].rearrange("p (g k) -> p g k", k=PK)
        i16 = spare[:, 1280:1536].bitcast(U32).rearrange("p (g k) -> p g k", k=PK)
        f16 = Hb[:, 2048:2304].rearrange("p (g k) -> p g k", k=PK)
        sv = Hb[:, 2304:2432].rearrange("p (g k) -> p g k", k=PK)
        si = Hb[:, 2432:2560].bitcast(U32).rearrange("p (g k) -> p g k", k=PK)
        ab = Hb[:, 2560:2816].bitcast(U32).rearrange("p (a n) -> p a n", a=2)
        abf = Hb[:, 2816:3072].rearrange("p (a n) -> p a n", a=2)
        pick = Hb[:, 3072:3328].rearrange("p (a n) -> p a n", a=2)
        so = h1[:, 0:256].rearrange("p (g n) -> p g n", g=2)

        s32 = dec[0:NS, 512:512 + 428]
        s128 = dec[:, 0:512]
        knew = sb("knew", [P, 2, NS])
        pt = sb("pt", [P, NB], I32)
        ptf = sb("ptf", [P, NB])
        gi = sb("gi", [P, NB], I32)
        qiS = spare[0:HD, 0:256].rearrange("p (b h t) -> p b h t", b=NB, h=HA)
        qaS = spare[:, 256:512].rearrange("p (b h t) -> p b h t", b=NB, h=HA)
        qrS = spare[:, 512:640].rearrange("p (h n) -> p h n", h=HR)
        krS = spare[:, 640:768].rearrange("p (h n) -> p h n", h=HR)
        wiS = spare[0:NS, 768:1024]
        qdm = spare[:, 1024:2048].rearrange("p (b h n) -> p b h n", b=NB, h=HR)
        qpad = S[0:NS, 0:1024].rearrange("p (h c d) -> p h c d", h=HA, c=KVH)

        psum = [ctx.enter_context(nc.psum_tensor(f"bank{i}", [P, 512], F32)) for i in range(6)]
        yacc = ctx.enter_context(nc.psum_tensor("yacc", [P, 1024], F32))
        full = [sem(f"full{i}") for i in range(6)]
        free = [sem(f"free{i}") for i in range(6)]

        def where(name):
            if name in short:
                return short[name]
            b, u = long[name]
            return 4 + b, u

        def bank(name):
            return psum[where(name)[0]]

        def claim(name):
            b, u = where(name)
            if u:
                nc.tensor.wait_ge(free[b], u)
            return psum[b]

        def fill(ins, name):
            ins.then_inc(full[where(name)[0]], 1)

        def filled(eng, name):
            b, u = where(name)
            eng.wait_ge(full[b], u + 1)
            return psum[b]

        def release(ins, name):
            ins.then_inc(free[where(name)[0]], 1)

        def released(eng, name):
            b, u = where(name)
            eng.wait_ge(free[b], u + 1)

        consts_in = sem("consts_in")
        tables_in = sem("tables_in")
        x_in = [sem("x_in0"), sem("x_in1")]
        win_in = sem("win_in")
        weights_in = sem("weights_in")
        x_scaled = sem("x_scaled")
        xT_ready = sem("xT_ready")
        h_ready = sem("h_ready")
        rotated = sem("rotated")
        h_stored = [sem("h_stored0"), sem("h_stored1")]
        keys_kept = sem("keys_kept")
        h_in = sem("h_in")
        residual_in = sem("residual_in")
        qi_ready = sem("qi_ready")
        qa_ready = sem("qa_ready")
        qr_ready = sem("qr_ready")
        kr_ready = sem("kr_ready")
        decayed_ready = sem("decayed_ready")
        qd_ready = sem("qd_ready")
        kd_ready = sem("kd_ready")
        state_ready = sem("state_ready")
        relu_ready = sem("relu_ready")
        relu_used = sem("relu_used")
        mask_ready = sem("mask_ready")
        logits_ready = sem("logits_ready")
        probs_ready = sem("probs_ready")
        pT_ready = sem("pT_ready")
        pT_used = sem("pT_used")
        exp_g = sem("exp_g")
        mix_ready = sem("mix_ready")
        mixT_ready = sem("mixT_ready")
        h1_ready = sem("h1_ready")
        xn_ready = sem("xn_ready")
        nT_ready = sem("nT_ready")
        peerq_ready = sem("peerq_ready")
        keys_ready = sem("keys_ready")
        gate_shifted = sem("gate_shifted")
        gate_exp = sem("gate_exp")
        chosen = sem("chosen")
        seeded = sem("seeded")
        row_in = [sem(f"row_in{i}") for i in range(RING)]
        row_used = sem("row_used")
        idx_ready = sem("idx_ready")
        slot_granted = sem("slot_granted")
        hval_ready = sem("hval_ready")
        gelu_ready = sem("gelu_ready")
        coef_ready = sem("coef_ready")
        diag_ready = sem("diag_ready")
        y_scaled = sem("y_scaled")
        norm_in = sem("norm_in")
        sconsts_in = sem("sconsts_in")
        stored = sem("stored")
        dve_chain = sem("dve_chain")
        act_chain = sem("act_chain")
        gated = sem("gated")
        states_in = sem("states_in")
        qpad_ready = sem("qpad_ready")
        wi_spread = sem("wi_spread")
        wiS_ready = sem("wiS_ready")
        kdm_ready = sem("kdm_ready")
        states_new = sem("states_new")
        states_out = sem("states_out")
        gi_ready = sem("gi_ready")
        g_in = sem("g_in")
        g_used = sem("g_used")
        skT_ready = sem("skT_ready")
        srelu_ready = sem("srelu_ready")
        slog_ready = sem("slog_ready")
        smax_ready = sem("smax_ready")
        sexp_ready = sem("sexp_ready")
        spT_ready = sem("spT_ready")
        so_ready = sem("so_ready")
        so_out = sem("so_out")
        att_in = sem("att_in")

        block = ctx.enter_context(nc.Block())
        NSTORE = [0]

        @block.sync
        def _(sp):
            def store(dst, src):
                sp.dma_start(dst, src).then_inc(stored, 16)
                NSTORE[0] += 1

            def load_x(t):
                R = rows(t)
                if t >= 2:
                    sp.wait_ge(full[short[("xT", t - 2, 1)][0]], short[("xT", t - 2, 1)][1] + 1)
                    sp.wait_ge(rotated, t - 1)
                sp.dma_start(xa[t % 2][0:R, :], x_of(t)).then_inc(x_in[t % 2], 16)
                sp.dma_start(rot[t % 2][0:R, :], c_rope[t * P:t * P + R, :]).then_inc(x_in[t % 2], 16)

            sp.dma_start(main[:], c_main).then_inc(consts_in, 16)
            sp.dma_start(colw[:], cols).then_inc(consts_in, 16)
            load_x(0)
            for k in range(KC):
                sp.dma_start(win[:, k, :], w_in[k * P:(k + 1) * P, :]).then_inc(win_in, 16)
            load_x(1)
            sp.dma_start(dec[:], c_dec).then_inc(tables_in, 16)
            sp.dma_start(keysT[:], sk).then_inc(tables_in, 16)
            sp.dma_start(pt[:], pages).then_inc(tables_in, 16)
            for what, n in schedule:
                if what == "project":
                    t, R = n, rows(n)
                    sp.wait_ge(rotated, t + 1)
                    r0 = t * P
                    sp.dma_start(h_dram[r0:r0 + R, :], H[t % 2][0:R, :]).then_inc(h_stored[t % 2], 16)
                    ko, vo, io = (k_p, v_p, ik_p) if t < TILES else (k_s, v_s, ik_s)
                    o0 = r0 if t < TILES else 0
                    for dst, c0, w in ((ko, KA, 128), (vo, VA, 128), (io, KI, 64)):
                        sp.dma_start(dst[o0:o0 + R, :], H[t % 2][0:R, c0:c0 + w]).then_inc(h_stored[t % 2], 16)
                    if t + 2 <= TILES:
                        load_x(t + 2)
                    if t == TILES:
                        sp.wait_ge(h_ready, TILES + 1)
                        sp.wait_ge(rotated, TILES + 1)
                        sp.dma_start(wout_sb[:], w_out.rearrange("(k p) n -> p k n", p=P)).then_inc(weights_in, 16)
                        sp.dma_start(wq_sb[:], w_q.rearrange("(k p) n -> p k n", p=P)).then_inc(weights_in, 16)
                elif what in ("heads", "sheads"):
                    t, R = n, rows(n)
                    sp.wait_ge(h_stored[0], 64 * 5)
                    sp.wait_ge(h_stored[1], 64 * 4)
                    sp.wait_ge(keys_kept, TILES + 1)
                    if t:
                        sp.wait_ge(chosen, t)
                    sp.dma_start(Hb[0:R, :], h_dram[t * P:t * P + R, :]).then_inc(h_in, 16)
                    if what == "sheads":
                        sp.wait_ge(qd_ready, TILES)
                        sp.dma_start(s128, c_s128).then_inc(sconsts_in, 16)
                        sp.dma_start(s32, c_s32).then_inc(sconsts_in, 16)
                        sp.wait_ge(mix_ready, TILES)
                        sp.dma_start(states[:], state_in).then_inc(states_in, 16)
                        sp.wait_ge(states_new, NB)
                        sp.dma_start(st_s, states[:]).then_inc(states_out, 16)
                        sp.dma_start(st_p, state[:].rearrange("p h e -> p (h e)")).then_inc(stored, 16)
                        NSTORE[0] += 1
                elif what == "sattend":
                    for g in range(2):
                        sp.wait_ge(so_ready, g + 1)
                        for bb in range(4):
                            for c in range(KVH):
                                r0 = ((4 * g + bb) * HA + 4 * c) * NT
                                p0 = 32 * bb + 16 * c
                                sp.dma_start(a_dram[r0:r0 + 16, :], so[p0:p0 + 16, g, c * HD:(c + 1) * HD]).then_inc(so_out, 16)
                    sp.wait_ge(so_out, 16 * 16)
                    for b in range(NB):
                        dst = Hb[4 * b:4 * b + 4, 0:512].rearrange("p (g c d) -> p g c d", c=KVH, d=HD)
                        for c in range(KVH):
                            src = a_dram[b * 32 + 16 * c:b * 32 + 16 * (c + 1), :].rearrange("(g t) d -> t g d", t=NT)
                            sp.dma_start(dst[:, :, c, :], src).then_inc(att_in, 16)
                elif what == "output":
                    t, R = n, rows(n)
                    if t:
                        sp.wait_ge(seeded, t)
                    if t == SAMPLE:
                        sp.wait_ge(so_out, 16 * 16)
                    sp.dma_start(h1[0:R, :], x_of(t)).then_inc(residual_in, 16)
                    if t >= 2:
                        sp.wait_ge(stored, 16 * NSTORE[0])
                    sp.dma_start(nw[:], wffn.partition_broadcast(P)).then_inc(norm_in, 16)
                elif what == "finish":
                    t, R = n, rows(n)
                    if t == SAMPLE:
                        sp.wait_ge(stored, 16 * NSTORE[0])
                    else:
                        sp.wait_ge(xn_ready, t + 2)
                    sp.dma_start(nw[:], wfin.partition_broadcast(P)).then_inc(norm_in, 16)
                    sp.wait_ge(y_scaled, t + 1)
                    store(y_p[t * P:t * P + R, :] if t < TILES else y_s, nw[0:R, :])
            sp.wait_ge(stored, 16 * NSTORE[0])
            sp.wait_ge(states_out, 16)

        @block.tensor
        def _(pe):
            pe.sem_inc(row_used, RING)

            def turn_x(t):
                R = rows(t)
                pe.wait_ge(x_in[t % 2], 32 * (t // 2 + 1))
                for g in range(2):
                    b = claim(("xT", t, g))
                    for k in range(4):
                        c = (4 * g + k) * P
                        mm = nc.tensor.transpose(b[:, k * R:(k + 1) * R], xa[t % 2][0:R, c:c + P], ident[0:R, 0:R])
                    fill(mm, ("xT", t, g))

            def turn_keys(t):
                R = rows(t)
                pe.wait_ge(rotated, t + 1)
                b = claim(("keysT", t))
                h = H[t % 2]
                nc.tensor.transpose(b[:, 0:R], h[0:R, KA:KA + 128], ident[0:R, 0:R])
                mm = nc.tensor.transpose(b[:, 128:128 + R], xn[0:R, t % 2, 0:128], ident[0:R, 0:R])
                fill(mm, ("keysT", t))

            def project(t):
                R = rows(t)
                if t == 0:
                    pe.wait_ge(consts_in, 32)
                    turn_x(0)
                if t < SAMPLE:
                    turn_x(t + 1)
                pe.wait_ge(xT_ready, t + 1)
                for n in range(7):
                    w = min(512, INW - 512 * n)
                    b = claim(("proj", t, n))
                    for k in range(KC):
                        if t == 0 and n == 0 and k == 0:
                            pe.wait_ge(win_in, 16 * KC)
                        mm = nc.tensor.matmul(b[0:R, 0:w], xT[t % 2][:, k, 0:R], win[:, k, 512 * n:512 * n + w],
                                              start=(k == 0), stop=(k == KC - 1))
                    fill(mm, ("proj", t, n))
                if t:
                    turn_keys(t - 1)
                if t == SAMPLE:
                    turn_keys(t)

            def turn_heads(t):
                pe.wait_ge(h_in, 16 * (t + 1))
                for name, c0 in (("qiT", QI), ("qaT", QA), ("qrT", QR), ("krT", KR)):
                    b = claim((name, t))
                    for g in range(4):
                        mm = nc.tensor.transpose(b[:, g * P:(g + 1) * P], Hb[:, c0 + g * P:c0 + (g + 1) * P], ident)
                    fill(mm, (name, t))

            def heads(t):
                turn_heads(t)
                pe.wait_ge(qr_ready, t + 1)
                pe.wait_ge(kr_ready, t + 1)
                b = claim(("decayed", t))
                for h in range(HR):
                    mm = nc.tensor.matmul(b[:, h * P:(h + 1) * P], krT[:, h, :], qrT[:, h, :], start=True, stop=True)
                fill(mm, ("decayed", t))
                pe.wait_ge(qd_ready, t + 1)
                if t:
                    pe.wait_ge(state_ready, t)
                o = claim(("ret", t))
                for h in range(HR):
                    v = Hb[:, VR + h * RD:VR + (h + 1) * RD]
                    nc.tensor.matmul(o[:, h * RD:(h + 1) * RD], krT[:, h, :], v, start=True, stop=False)
                    mm = nc.tensor.matmul(o[:, h * RD:(h + 1) * RD], qrT[:, h, :], state[:, h, :], start=False, stop=True)
                fill(mm, ("ret", t))
                pe.wait_ge(kd_ready, t + 1)
                b = claim(("state", t))
                for h in range(HR):
                    mm = nc.tensor.matmul(b[:, h * RD:(h + 1) * RD], Hb[:, KR + h * RD:KR + (h + 1) * RD],
                                          Hb[:, VR + h * RD:VR + (h + 1) * RD], start=True, stop=True)
                fill(mm, ("state", t))

            def scores(t):
                pe.wait_ge(qi_ready, t + 1)
                for c in range((t + 4) // 4):
                    w = min(512, (t + 1) * P - 512 * c)
                    for h in range(HI):
                        p0 = 64 * (h % 2)
                        b = claim(("score", t, c, h))
                        mm = nc.tensor.matmul(b[:, 0:w], qiT[p0:p0 + 64, h // 2, :], kiT[p0:p0 + 64, 512 * c:512 * c + w],
                                              start=True, stop=True)
                        fill(mm, ("score", t, c, h))

            def attend(t):
                nch = (t + 4) // 4
                pe.wait_ge(qa_ready, t + 1)
                o = claim(("att", t))
                for h in range(HA + 1):
                    if h < HA:
                        p0 = 64 * (h % 2)
                        for c in range(nch):
                            w = min(512, (t + 1) * P - 512 * c)
                            b = claim(("logit", t, h, c))
                            mm = nc.tensor.matmul(b[:, 0:w], qaT[p0:p0 + 64, h // 2, :], kT[p0:p0 + 64, 512 * c:512 * c + w],
                                                  start=True, stop=True)
                            fill(mm, ("logit", t, h, c))
                    if h:
                        g = h - 1
                        pe.wait_ge(probs_ready, 8 * t + g + 1)
                        for c in range(nch):
                            n = min(4, t + 1 - 4 * c)
                            b = claim(("pT", t, g, c))
                            for k in range(n):
                                col = 1024 * (g % 2) + (4 * c + k) * P
                                mm = nc.tensor.transpose(b[:, k * P:(k + 1) * P], S[:, col:col + P], ident)
                            fill(mm, ("pT", t, g, c))
                        for c in range(nch):
                            n = min(4, t + 1 - 4 * c)
                            m = turned_no[(t, g, c)]
                            pe.wait_ge(pT_ready, m + 1)
                            for k in range(n):
                                kt = 4 * c + k
                                mm = nc.tensor.matmul(o[:, g * HD:(g + 1) * HD], mid[:, m % 2, k * P:(k + 1) * P],
                                                      vall[:, kt, HD * (g % 2):HD * (g % 2) + HD],
                                                      start=(kt == 0), stop=(kt == t))
                            if not (c == nch - 1 and g == HA - 1):
                                mm.then_inc(pT_used, 1)
                fill(mm, ("att", t))

            def output(t):
                R = rows(t)
                pe.wait_ge(mix_ready, t + 1)
                if t == SAMPLE:
                    pe.wait_ge(att_in, 16 * NB * KVH)
                if t == 0:
                    pe.wait_ge(weights_in, 32)
                for g in range(2):
                    b = claim(("mixT", t, g))
                    for k in range(4):
                        c = (0 if g == 0 else GR) + k * P
                        mm = nc.tensor.transpose(b[:, k * R:(k + 1) * R], Hb[0:R, c:c + P], ident[0:R, 0:R])
                    fill(mm, ("mixT", t, g))
                pe.wait_ge(mixT_ready, t + 1)
                mixT = spare[:, 0:1024].rearrange("p (k n) -> p k n", k=KC)
                for n in range(2):
                    b = claim(("out", t, n))
                    for k in range(KC):
                        mm = nc.tensor.matmul(b[0:R, :], mixT[:, k, 0:R], wout_sb[:, k, 512 * n:512 * (n + 1)],
                                              start=(k == 0), stop=(k == KC - 1))
                    fill(mm, ("out", t, n))
                pe.wait_ge(xn_ready, t + 1)
                for g in range(2):
                    b = claim(("nT", t, g))
                    for k in range(4):
                        c = (4 * g + k) * P
                        mm = nc.tensor.transpose(b[:, k * R:(k + 1) * R], xn[0:R, t % 2, c:c + P], ident[0:R, 0:R])
                    fill(mm, ("nT", t, g))
                pe.wait_ge(nT_ready, t + 1)
                nT = spare[:, 1024:2048].rearrange("p (k n) -> p k n", k=KC)
                for g in range(2):
                    b = claim(("peerq", t, g))
                    for h in range(4 * g, 4 * g + 4):
                        for k in range(KC):
                            mm = nc.tensor.matmul(b[:, (h % 4) * R:(h % 4 + 1) * R], wq_sb[:, k, h * P:(h + 1) * P], nT[:, k, 0:R],
                                                  start=(k == 0), stop=(k == KC - 1))
                    fill(mm, ("peerq", t, g))
                pe.wait_ge(peerq_ready, t + 1)
                for n in range(4):
                    b = claim(("keys", t, n))
                    for h in (2 * n, 2 * n + 1):
                        mm = nc.tensor.matmul(b[0:R, (h % 2) * 256:(h % 2 + 1) * 256], mixT[:, h, 0:R], keysT[:, :],
                                              start=True, stop=True)
                    fill(mm, ("keys", t, n))

            def seed(t):
                R = rows(t)
                pe.wait_ge(h1_ready, t + 1)
                if t:
                    pe.wait_ge(y_scaled, t)
                for j in range(2):
                    mm = nc.tensor.matmul(yacc[:, 512 * j:512 * (j + 1)], ident[0:R, :], h1[0:R, 512 * j:512 * (j + 1)],
                                          start=True, stop=False, skip_group_check=True)
                mm.then_inc(seeded, 1)

            def peer(t, head):
                R = rows(t)
                with pe.Fori(0, 2) as i:
                    for s in range(8):
                        n0 = 8 * 2 * head
                        pe.wait_ge(diag_ready, i * 8 + (n0 + s + 1))
                        for j in range(2):
                            mm = nc.tensor.matmul(yacc[:, 512 * j:512 * (j + 1)], diag[0:R, s % 4, :],
                                                  ring[0:R, s, D + 512 * j:D + 512 * (j + 1)],
                                                  start=False, stop=False, skip_group_check=True)
                        mm.then_inc(row_used, 1)

            def sheads(t):
                pe.wait_ge(h_in, 16 * (t + 1))
                pe.wait_ge(qpad_ready, 1)
                b = claim(("qiT", t))
                for h in range(HI):
                    mm = nc.tensor.transpose(b[0:HD, h * NS:(h + 1) * NS], Hb[0:NS, QI + h * HD:QI + (h + 1) * HD], ident[0:NS, 0:NS])
                fill(mm, ("qiT", t))
                b = claim(("qaT", t))
                for h in range(HA):
                    mm = nc.tensor.transpose(b[:, h * NS:(h + 1) * NS], qpad[:, h, :, :].rearrange("p c d -> p (c d)"), ident[0:NS, 0:NS])
                fill(mm, ("qaT", t))
                for name, c0 in (("qrT", QR), ("krT", KR)):
                    b = claim((name, t))
                    for g in range(4):
                        mm = nc.tensor.transpose(b[:, g * NS:(g + 1) * NS], Hb[0:NS, c0 + g * P:c0 + (g + 1) * P], ident[0:NS, 0:NS])
                    fill(mm, (name, t))
                pe.wait_ge(qr_ready, t + 1)
                pe.wait_ge(kr_ready, t + 1)
                b = claim(("decayed", t))
                for h in range(HR):
                    mm = nc.tensor.matmul(b[0:NS, h * NS:(h + 1) * NS], krS[:, h, :], qrS[:, h, :], start=True, stop=True)
                fill(mm, ("decayed", t))
                pe.wait_ge(wi_spread, 1)
                b = claim(("wiT", t))
                for k in range(NB):
                    mm = nc.tensor.transpose(b[0:NS, k * NS:(k + 1) * NS], S[0:NS, 1024 + k * NS:1024 + (k + 1) * NS], ident[0:NS, 0:NS])
                fill(mm, ("wiT", t))
                pe.wait_ge(qd_ready, t + 1)
                pe.wait_ge(states_in, 16)
                o = claim(("ret", t))
                for h in range(HR):
                    oh = o[0:NS, h * RD:(h + 1) * RD]
                    nc.tensor.matmul(oh, S[0:NS, 1280 + h * NS:1280 + (h + 1) * NS], Hb[0:NS, VR + h * RD:VR + (h + 1) * RD],
                                     start=True, stop=False)
                    for k in range(NB):
                        mm = nc.tensor.matmul(oh, qdm[:, k, h, :], states[:, k, h, :], start=False, stop=(k == NB - 1))
                fill(mm, ("ret", t))
                for k in range(NB):
                    pe.wait_ge(kdm_ready, k + 1)
                    b = claim(("sstate", k))
                    for h in range(HR):
                        mm = nc.tensor.matmul(b[:, h * RD:(h + 1) * RD], mid[0:NS, k % 2, h * RD:(h + 1) * RD],
                                              Hb[0:NS, VR + h * RD:VR + (h + 1) * RD], start=True, stop=True)
                    fill(mm, ("sstate", k))

            def sscores():
                pe.wait_ge(qi_ready, SAMPLE + 1)
                pe.wait_ge(wiS_ready, 1)
                kc = mid[0:HD, 0, :]
                for b_ in range(NB):
                    pe.wait_ge(g_in, 16 * (b_ + 1))
                    for c in range(5):
                        m = 5 * b_ + c
                        w = 512 if c < 4 else NS
                        if c < 4:
                            b = claim(("skT", b_, c))
                            for k in range(4):
                                mm = nc.tensor.transpose(b[0:HD, k * P:(k + 1) * P], G[:, (4 * c + k) * HD:(4 * c + k + 1) * HD], ident)
                            fill(mm, ("skT", b_, c))
                            pe.wait_ge(skT_ready, 4 * b_ + c + 1)
                            rhs = kc
                        else:
                            rhs = knew[0:HD, 1, :]
                        b = claim(("sdot", b_, c))
                        mm = nc.tensor.matmul(b[0:NS, 0:w], qiS[:, b_, :, :].rearrange("p h t -> p (h t)"), rhs, start=True, stop=True)
                        fill(mm, ("sdot", b_, c))
                        pe.wait_ge(srelu_ready, m + 1)
                        b = claim(("ssum", b_, c))
                        mm = nc.tensor.matmul(b[0:NS, 0:w], wiS[:, b_ * NS:(b_ + 1) * NS], mid[0:NS, 1, 0:w], start=True, stop=True)
                        fill(mm, ("ssum", b_, c))

            def sattend():
                pe.wait_ge(qa_ready, SAMPLE + 1)
                pe.wait_ge(mask_ready, SAMPLE + 1)
                for g in range(2):
                    for bb in range(4):
                        b_ = 4 * g + bb
                        pe.wait_ge(g_in, 16 * (NB + 8 * g + bb + 1))
                        q = qaS[:, b_, :, :].rearrange("p h t -> p (h t)")
                        rep = s32[:, 140 + b_ * NS:140 + (b_ + 1) * NS]
                        for c in range(5):
                            w = 512 if c < 4 else NS
                            if c < 4:
                                b = claim(("sKT", b_, c))
                                for k in range(4):
                                    mm = nc.tensor.transpose(b[:, k * P:(k + 1) * P], G[:, (4 * c + k) * P:(4 * c + k + 1) * P], ident)
                                fill(mm, ("sKT", b_, c))
                                pe.wait_ge(skT_ready, 32 + 4 * b_ + c + 1)
                                rhs = mid[:, c % 2, :]
                                neg = scs[:, 0:PAST].rearrange("q (p k) -> q k p", k=BLK)[:, 4 * c:4 * c + 4, :]
                            else:
                                rhs, neg = knew[:, 0, :], scs[:, PAST:SL]
                            b = claim(("slog", b_, c))
                            ob = b[32 * bb:32 * bb + 32, 0:w]
                            nc.tensor.matmul(ob, q, rhs, start=True, stop=False)
                            ob2 = ob.rearrange("q (k p) -> q k p", p=P) if c < 4 else ob
                            mm = nc.tensor.matmul(ob2, rep, neg, start=False, stop=True)
                            fill(mm, ("slog", b_, c))
                    pe.wait_ge(sexp_ready, g + 1)
                    pTs = Hb[:, 768:2816].rearrange("p (k n) -> p k n", k=BLK)
                    for c in range(5):
                        b = claim(("spT", g, c))
                        if c < 4:
                            for k in range(4):
                                mm = nc.tensor.transpose(b[:, k * P:(k + 1) * P], S[:, (4 * c + k) * P:(4 * c + k + 1) * P], ident)
                        else:
                            mm = nc.tensor.transpose(b[0:NS, 0:P], S[:, PAST:SL], ident)
                        fill(mm, ("spT", g, c))
                    pe.wait_ge(spT_ready, g + 1)
                    o = claim(("satt", g))
                    for bb in range(4):
                        pe.wait_ge(g_in, 16 * (NB + 8 * g + 4 + bb + 1))
                        ob = o[32 * bb:32 * bb + 32, 0:P]
                        for k in range(BLK):
                            mm = nc.tensor.matmul(ob, pTs[:, k, 32 * bb:32 * bb + 32], G[:, k * P:(k + 1) * P], start=(k == 0), stop=False)
                        mm.then_inc(g_used, 1)
                        mm = nc.tensor.matmul(ob, knewp[:, 32 * bb:32 * bb + 32], Hb[0:NS, VA:VA + P], start=False, stop=True)
                    fill(mm, ("satt", g))

            knewp = wiS[:, 0:P]
            steps = {"project": project, "heads": heads, "scores": scores, "attend": attend, "output": output,
                     "seed": seed, "sheads": sheads}
            for what, n in schedule:
                if what == "peer":
                    peer(n // 8, n)
                elif what == "sscores":
                    sscores()
                elif what == "sattend":
                    sattend()
                elif what == "finish":
                    pass
                elif what in steps:
                    steps[what](n)

        @block.vector
        def _(dve):
            V = nc.vector
            count = [0]

            def link(ins):
                count[0] += 1
                ins.then_inc(dve_chain, 1)
                dve.wait_ge(dve_chain, count[0])

            def tt(o, a, b, op):
                link(V.tensor_tensor(o, a, b, op))

            def inverse_root(dst, src, R, w):
                y, a = tiny[0:R, 58:58 + w], tinyb[0:R, 0:w]
                link(V.tensor_scalar(y.bitcast(I32), src.bitcast(I32), -0.5, float(0x5F3759DF), ALU.mult, ALU.add))
                for k in range(3):
                    tt(a, y, y, ALU.mult)
                    tt(a, a, src, ALU.mult)
                    link(V.tensor_scalar(a, a, -0.5, 1.5, ALU.mult, ALU.add))
                    if k < 2:
                        tt(y, y, a, ALU.mult)
                return V.tensor_tensor(dst, y, a, ALU.mult)

            def inverse_rms(dst, src, R):
                st = tiny[0:R, 8:20]
                for j in range(2):
                    link(V.bn_stats(st[:, 6 * j:6 * j + 6], src[0:R, 512 * j:512 * (j + 1)]))
                link(V.bn_aggr(tiny[0:R, 20:22], st))
                link(V.scalar_tensor_tensor(tiny[0:R, 22:23], tiny[0:R, 20:21], tiny[0:R, 20:21], tiny[0:R, 21:22], ALU.mult, ALU.add))
                link(V.tensor_scalar(tiny[0:R, 22:23], tiny[0:R, 22:23], EPS, None, ALU.add))
                return inverse_root(dst, tiny[0:R, 22:23], R, 1)

            def scale_x(t):
                R = rows(t)
                dve.wait_ge(x_in[t % 2], 32 * (t // 2 + 1))
                inverse_rms(tiny[0:R, t % 2:t % 2 + 1], xa[t % 2], R).then_inc(x_scaled, 1)

            def rotate(h, c0, n, hd, half, cos, sin, R):
                x = h[0:R, c0:c0 + n * hd].rearrange("p (n d) -> p n d", n=n)
                x1, x2 = x[:, :, 0:half], x[:, :, half:2 * half]
                cb = cos[0:R, None, :].broadcast_to((R, n, half))
                sb_ = sin[0:R, None, :].broadcast_to((R, n, half))
                t4 = [rt[0:R, a, 0:n * half].rearrange("p (n d) -> p n d", n=n) for a in range(4)]
                V.tensor_tensor(t4[0], x1, cb, ALU.mult)
                V.tensor_tensor(t4[1], x2, sb_, ALU.mult)
                V.tensor_tensor(t4[2], x2, cb, ALU.mult)
                link(V.tensor_tensor(t4[3], x1, sb_, ALU.mult))
                V.tensor_tensor(x1, t4[0], t4[1], ALU.subtract)
                return V.tensor_tensor(x2, t4[2], t4[3], ALU.add)

            def project(t):
                R = rows(t)
                if t == 0:
                    link(V.memset(state[:], 0.0))
                    scale_x(0)
                if t < SAMPLE:
                    scale_x(t + 1)
                dve.wait_ge(h_ready, t + 1)
                dve.wait_ge(x_in[t % 2], 32 * (t // 2 + 1))
                r, h = rot[t % 2], H[t % 2]
                link(rotate(h, QA, HA + KVH, HD, 8, r[:, 0:8], r[:, 8:16], R))
                link(rotate(h, QI, HI + 1, HD, 8, r[:, 0:8], r[:, 8:16], R))
                link(rotate(h, QR, 2 * HR, RD, 64, r[:, 16:80], r[:, 80:144], R))
                link(V.tensor_scalar(h[0:R, WI:WI + HI], h[0:R, WI:WI + HI], HI ** -0.5 * HD ** -0.5, None, ALU.mult))
                if t < TILES:
                    V.tensor_copy(vall[:, t, :], h[:, VA:VA + 128])
                ki2 = h[0:R, None, KI:KI + HD].broadcast_to((R, 2, HD))
                V.tensor_copy(xn[0:R, t % 2, 0:128].rearrange("p (a d) -> p a d", a=2), ki2).then_inc(rotated, 1)

            def retention_out(t, gate_sem):
                R = rows(t)
                o = filled(dve, ("ret", t))
                for h in range(HR):
                    link(V.bn_stats(tiny[0:R, 8:14], o[0:R, h * RD:(h + 1) * RD]))
                    link(V.bn_aggr(tiny[0:R, 24 + 2 * h:26 + 2 * h], tiny[0:R, 8:14]))
                ms = tiny[0:R, 24:32].rearrange("p (h a) -> p h a", a=2)
                link(V.tensor_scalar(tiny[0:R, 32:36], ms[:, :, 1], EPS, None, ALU.add))
                link(inverse_root(tiny[0:R, 32:36], tiny[0:R, 32:36], R, HR))
                on = Hb[0:R, QR:QR + 512]
                for h in range(HR):
                    ins = V.tensor_scalar(on[:, h * RD:(h + 1) * RD], o[0:R, h * RD:(h + 1) * RD], tiny[0:R, 24 + 2 * h:25 + 2 * h],
                                          tiny[0:R, 32 + h:33 + h], ALU.subtract, ALU.mult)
                    if h < HR - 1:
                        link(ins)
                release(ins, ("ret", t))
                released(dve, ("ret", t))
                g = Hb[0:R, GR:GR + 512]
                dve.wait_ge(exp_g, t + 1)
                e = Hb[0:R, KR:KR + 512]
                link(V.tensor_scalar(e, e, 1.0, None, ALU.add))
                link(V.reciprocal(e, e))
                tt(g, g, e, ALU.mult)
                V.tensor_tensor(g, g, on, ALU.mult).then_inc(gated, 1)

            def heads(t):
                dve.wait_ge(h_in, 16 * (t + 1))
                dve.wait_ge(tables_in, 48)
                b = filled(dve, ("decayed", t))
                release(V.tensor_tensor(krT[:].rearrange("p g n -> p (g n)"), b[:, :], dec[:, 0:512], ALU.mult), ("decayed", t))
                V.tensor_tensor(qrT[:].rearrange("p g n -> p (g n)"), qrT[:].rearrange("p g n -> p (g n)"),
                                dec[:, 512:1024], ALU.mult).then_inc(qd_ready, 1)
                filled(dve, ("krT", t))
                kr = Hb[:, KR:KR + 512].rearrange("p (h d) -> p h d", h=HR)
                V.tensor_tensor(kr, kr, main[:, 272:276, None].broadcast_to((P, HR, RD)), ALU.mult).then_inc(kd_ready, 1)
                b = filled(dve, ("state", t))
                for h in range(HR):
                    ins = V.scalar_tensor_tensor(state[:, h, :], state[:, h, :], float(np.exp(LOGG[h] * P)),
                                                 b[:, h * RD:(h + 1) * RD], ALU.mult, ALU.add)
                    if h < HR - 1:
                        link(ins)
                release(ins, ("state", t))
                released(dve, ("state", t))
                V.memset(tiny[0:1, 37:38], 0.0).then_inc(state_ready, 1)
                retention_out(t, None)

            def scores(t):
                for c in range((t + 4) // 4):
                    w = min(512, (t + 1) * P - 512 * c)
                    for h in range(HI):
                        m = score_no[(t, c, h)]
                        dve.wait_ge(relu_ready, m + 1)
                        d = sc[:, 512 * c:512 * c + w]
                        wi = Hb[:, WI + h:WI + h + 1]
                        if h == 0:
                            V.tensor_scalar(d, mid[:, m % 2, 0:w], wi, None, ALU.mult).then_inc(relu_used, 1)
                        else:
                            V.scalar_tensor_tensor(d, mid[:, m % 2, 0:w], wi, d, ALU.mult, ALU.add).then_inc(relu_used, 1)
                        dve.wait_ge(relu_used, m + 1)
                tt(sc[:, t * P:(t + 1) * P], sc[:, t * P:(t + 1) * P], causal, ALU.add)

            def topk(t, part):
                a = sc[:, 0:(t + 1) * P] if t < TILES else scs
                R = rows(t)
                if t == SAMPLE and part == 0:
                    tt(scs[:, PAST:SL], scs[:, PAST:SL], s32[:, 396:428], ALU.add)
                for _ in range(ROUNDS // 4):
                    link(V.max(tiny[0:R, 40:48], a))
                    link(V.match_replace(a, tiny[0:R, 40:48], a, CHOSEN))

            def mask(t):
                if t < 2:
                    if t:
                        link(V.memset(sc[:, 0:t * P], 0.0))
                    V.tensor_scalar(sc[:, t * P:(t + 1) * P], causal, -1.0, -BIG, ALU.is_lt, ALU.mult).then_inc(mask_ready, 1)
                else:
                    a = sc[:, 0:(t + 1) * P] if t < TILES else scs
                    V.tensor_scalar(a, a, -3.3e38, -BIG, ALU.is_gt, ALU.mult).then_inc(mask_ready, 1)
                dve.wait_ge(mask_ready, t + 1)

            def attend(t):
                nch = (t + 4) // 4
                for h in range(HA):
                    if h >= 2:
                        filled(dve, ("pT", t, h - 2, nch - 1))
                    for c in range(nch):
                        w = min(512, (t + 1) * P - 512 * c)
                        b = filled(dve, ("logit", t, h, c))
                        ins = V.tensor_tensor_reduce(S[:, 1024 * (h % 2) + 512 * c:1024 * (h % 2) + 512 * c + w], b[:, 0:w],
                                                     sc[:, 512 * c:512 * c + w], 1.0, -3.0e38, ALU.add, ALU.max,
                                                     tiny[:, 48 + c:49 + c])
                        release(ins, ("logit", t, h, c))
                    released(dve, ("logit", t, h, nch - 1))
                    if nch == 2:
                        tt(tiny[:, 48:49], tiny[:, 48:49], tiny[:, 49:50], ALU.max)
                    V.tensor_scalar(nmx[:, h:h + 1], tiny[:, 48:49], -HD ** -0.5, None, ALU.mult).then_inc(logits_ready, 1)
                    dve.wait_ge(logits_ready, 8 * t + h + 1)
                dve.wait_ge(probs_ready, 8 * (t + 1))
                link(V.reciprocal(tiny[:, 50:58], rs[:, 0:8]))
                o = filled(dve, ("att", t))
                dst = Hb[:, 0:512].rearrange("p (h d) -> p h d", h=HA)
                release(V.tensor_tensor(dst, o[:, :].rearrange("p (h d) -> p h d", h=HA),
                                        tiny[:, 50:58, None].broadcast_to((P, HA, HD)), ALU.mult), ("att", t))
                released(dve, ("att", t))
                V.memset(tiny[0:1, 36:37], 0.0).then_inc(mix_ready, 1)

            def output(t):
                R = rows(t)
                dve.wait_ge(residual_in, 16 * (t + 1))
                for n in range(2):
                    b = filled(dve, ("out", t, n))
                    release(V.tensor_tensor(h1[0:R, 512 * n:512 * (n + 1)], b[0:R, :], h1[0:R, 512 * n:512 * (n + 1)], ALU.add), ("out", t, n))
                    released(dve, ("out", t, n))
                inverse_rms(tiny[0:R, 2:3], h1, R).then_inc(h1_ready, 1)
                dve.wait_ge(h1_ready, t + 1)
                dve.wait_ge(norm_in, 16 * norm_no[("output", t)])
                V.scalar_tensor_tensor(xn[0:R, t % 2, :], h1[0:R, :], tiny[0:R, 2:3], nw[0:R, :], ALU.mult, ALU.mult).then_inc(xn_ready, 1)
                dve.wait_ge(xn_ready, t + 1)

            def top16(vals, idxs, a):
                link(V.max(vals[:, 0:8], a))
                link(V.max_index(idxs[:, 0:8], vals[:, 0:8], a))
                link(V.match_replace(a, vals[:, 0:8], a, CHOSEN))
                link(V.max(vals[:, 8:16], a))
                link(V.max_index(idxs[:, 8:16], vals[:, 8:16], a))

            def choose(t):
                R = rows(t)
                dve.wait_ge(keys_ready, t + 1)
                sx = Hb[0:R, 0:2048].rearrange("p (g n) -> p g n", g=16)
                for g in range(16):
                    top16(v16[0:R, g, :], i16[0:R, g, :], sx[:, g, :])
                link(V.tensor_copy(f16[0:R], i16[0:R]))
                cand = S[0:R, 0:2048].rearrange("p (h i j) -> p h i j", h=PH, i=PK)
                v4 = v16[0:R].rearrange("p (h a) k -> p h a k", a=2)
                f4 = f16[0:R].rearrange("p (h a) k -> p h a k", a=2)
                tt(cand, v4[:, :, 0, :, None].broadcast_to((R, PH, PK, PK)), v4[:, :, 1, None, :].broadcast_to((R, PH, PK, PK)), ALU.add)
                for h in range(PH):
                    top16(sv[0:R, h, :], si[0:R, h, :], S[0:R, 256 * h:256 * (h + 1)])
                g = gate[0:R, t % 2]
                V.tensor_tensor(g, sv[0:R], sv[0:R, :, 0:1].broadcast_to((R, PH, PK)), ALU.subtract).then_inc(gate_shifted, 1)
                siv = si[0:R].rearrange("p h k -> p (h k)")
                link(V.tensor_scalar(ab[0:R, 0, :], siv, 4, None, ALU.logical_shift_right))
                link(V.tensor_scalar(ab[0:R, 1, :], siv, 15, None, ALU.bitwise_and))
                link(V.tensor_copy(abf[0:R], ab[0:R]))
                eq = Hb[0:R, 0:2048].rearrange("p (n i) -> p n i", i=PK)
                eq4 = Hb[0:R, 0:2048].rearrange("p (h k i) -> p h k i", h=PH, i=PK)
                for a in range(2):
                    tt(eq, abf[0:R, a, :, None].broadcast_to((R, SLOTS, PK)), iota16[0:R, None, :].broadcast_to((R, SLOTS, PK)), ALU.is_equal)
                    tt(eq4, eq4, f4[:, :, a, None, :].broadcast_to((R, PH, PK, PK)), ALU.mult)
                    link(V.tensor_reduce(pick[0:R, a, :], eq, AX.X, ALU.add))
                link(V.scalar_tensor_tensor(abf[0:R, 0, :], pick[0:R, 0, :], float(NKEY), pick[0:R, 1, :], ALU.mult, ALU.add))
                link(V.tensor_copy(eid[0:R, t % 2, :], abf[0:R, 0, :]))
                dve.wait_ge(gate_exp, t + 1)
                link(V.tensor_reduce(tiny[0:R, 50:58], g, AX.X, ALU.add))
                link(V.reciprocal(tiny[0:R, 50:58], tiny[0:R, 50:58]))
                V.tensor_tensor(g, g, tiny[0:R, 50:58, None].broadcast_to((R, PH, PK)), ALU.mult).then_inc(chosen, 1)
                dve.wait_ge(chosen, t + 1)

            def peer(t, head):
                R = rows(t)
                h = head % PH
                gates = gate[:].rearrange("p a h k -> p (a h k)")
                with dve.Fori(0, 2) as i:
                    for j in range(2):
                        for s in range(4 * j, 4 * j + 4):
                            dve.wait_ge(row_in[s], i * 16 + 16 * (2 * head + 1))
                            u = ring[0:R, s, 0:D]
                            ins = V.tensor_tensor_reduce(u, u, xn[0:R, t % 2, :], 1.0, 0.0, ALU.mult, ALU.add, hv[0:R, s:s + 1])
                        ins.then_inc(hval_ready, 1)
                        dve.wait_ge(gelu_ready, i * 2 + (4 * head + j + 1))
                        col = (t % 2) * SLOTS + h * PK + 4 * j
                        V.tensor_tensor(coef[0:R, 4 * j:4 * j + 4], gl[0:R, 4 * j:4 * j + 4],
                                        gates[0:R, bass.ds(i * 8 + col, 4)], ALU.mult).then_inc(coef_ready, 1)

            def finish(t):
                R = rows(t)
                dve.wait_ge(row_used, RING + SLOTS * (t + 1))
                link(inverse_rms(tiny[0:R, 3:4], yacc, R))
                dve.wait_ge(norm_in, 16 * norm_no[("finish", t)])
                V.scalar_tensor_tensor(nw[0:R, :], yacc[0:R, :], tiny[0:R, 3:4], nw[0:R, :], ALU.mult, ALU.mult).then_inc(y_scaled, 1)

            def sheads(t):
                dve.wait_ge(h_in, 16 * (t + 1))
                dve.wait_ge(sconsts_in, 32)
                link(V.memset(S[0:NS, 0:1024], 0.0))
                q = Hb[0:NS, 0:512].rearrange("p (h d) -> p h d", h=HA)
                link(V.tensor_copy(qpad[:, 0:4, 0, :], q[:, 0:8:2, :]))
                V.tensor_copy(qpad[:, 4:8, 1, :], q[:, 1:8:2, :]).then_inc(qpad_ready, 1)
                rep = s32[:, 140:396].rearrange("p (b h t) -> p b h t", b=NB, h=HA)
                wsp = S[0:NS, 1024:1280].rearrange("p (b h t) -> p b h t", b=NB, h=HA)
                V.tensor_tensor(wsp, rep, Hb[0:NS, None, WI:WI + HI, None].broadcast_to((NS, NB, HA, NT)), ALU.mult).then_inc(wi_spread, 1)
                dve.wait_ge(wi_spread, 1)
                dve.wait_ge(qr_ready, t + 1)
                qf = spare[:, 512:640]
                b = filled(dve, ("decayed", t))
                release(V.tensor_tensor(S[0:NS, 1280:1408], b[0:NS, 0:128], s32[:, 0:128], ALU.mult), ("decayed", t))
                tt(qf, qf, s128[:, 0:128], ALU.mult)
                bm = s128[:, 128:384].rearrange("p (b n) -> p b n", b=NB)
                V.tensor_tensor(qdm, qrS[:, None, :, :].broadcast_to((P, NB, HR, NS)), bm[:, :, None, :].broadcast_to((P, NB, HR, NS)),
                                ALU.mult).then_inc(qd_ready, 1)
                filled(dve, ("krT", t))
                kr = Hb[0:NS, KR:KR + 512].rearrange("p (h d) -> p h d", h=HR)
                tt(kr, kr, s32[:, 128:132, None].broadcast_to((NS, HR, RD)), ALU.mult)
                for k in range(NB + 1):
                    if k < NB:
                        if k >= 2:
                            filled(dve, ("sstate", k - 2))
                        V.tensor_scalar(mid[0:NS, k % 2, :], Hb[0:NS, KR:KR + 512], s32[:, 132 + k:133 + k], None, ALU.mult).then_inc(kdm_ready, 1)
                    if k:
                        b = filled(dve, ("sstate", k - 1))
                        for h in range(HR):
                            ins = V.scalar_tensor_tensor(states[:, k - 1, h, :], states[:, k - 1, h, :], float(np.exp(LOGG[h] * NT)),
                                                         b[:, h * RD:(h + 1) * RD], ALU.mult, ALU.add)
                            if h < HR - 1:
                                link(ins)
                        release(ins, ("sstate", k - 1))
                        released(dve, ("sstate", k - 1))
                        V.memset(tiny[0:1, 36:37], 0.0).then_inc(states_new, 1)
                V.memset(tiny[0:1, 38:39], 0.0).then_inc(kd_ready, 1)
                dve.wait_ge(kd_ready, t + 1)
                retention_out(t, None)
                link(V.tensor_copy(ptf[:], pt[:]))
                link(V.tensor_scalar(ptf[:], ptf[:], 8.0, main[:, 276:277], ALU.mult, ALU.add))
                V.tensor_copy(gi[:], ptf[:]).then_inc(gi_ready, 1)

            def sscores():
                for b_ in range(NB):
                    for c in range(5):
                        p = filled(dve, ("ssum", b_, c))
                        if c < 4:
                            d = scs[:, 0:PAST].rearrange("q (p k) -> q k p", k=BLK)[:, 4 * c:4 * c + 4, :]
                            src = p[0:NS, 0:512].rearrange("q (k p) -> q k p", k=4)
                        else:
                            d, src = scs[:, PAST:SL], p[0:NS, 0:NS]
                        if b_ == 0:
                            ins = V.tensor_copy(d, src)
                        else:
                            ins = V.tensor_tensor(d, d, src, ALU.add)
                        release(ins, ("ssum", b_, c))
                        released(dve, ("ssum", b_, c))

            def sattend():
                for g in range(2):
                    dve.wait_ge(slog_ready, 20 * (g + 1))
                    link(V.tensor_reduce(tiny[:, 48:49], S[:, 0:SL], AX.X, ALU.max))
                    V.tensor_scalar(nmx[:, g:g + 1], tiny[:, 48:49], -HD ** -0.5, None, ALU.mult).then_inc(smax_ready, 1)
                    dve.wait_ge(sexp_ready, g + 1)
                    link(V.reciprocal(tiny[:, 50:51], rs[:, g:g + 1]))
                    o = filled(dve, ("satt", g))
                    release(V.scalar_tensor_tensor(so[:, g, :], o[:, 0:P], tiny[:, 50:51], s128[:, 384:512], ALU.mult, ALU.mult), ("satt", g))
                    released(dve, ("satt", g))
                    V.memset(tiny[0:1, 36:37], 0.0).then_inc(so_ready, 1)
                V.memset(tiny[0:1, 38:39], 0.0).then_inc(mix_ready, 1)

            steps = {"project": project, "heads": heads, "scores": scores, "mask": mask, "attend": attend, "output": output,
                     "choose": choose, "finish": finish, "sheads": sheads}
            for what, n in schedule:
                if what == "peer":
                    peer(n // 8, n)
                elif what == "topk":
                    topk(n // 4, n % 4)
                elif what == "sscores":
                    sscores()
                elif what == "sattend":
                    sattend()
                elif what in steps:
                    steps[what](n)

        @block.scalar
        def _(act):
            A = nc.scalar

            def project(t):
                R = rows(t)

                def scale_turned(u):
                    Ru = rows(u)
                    for g in range(2):
                        b = filled(act, ("xT", u, g))
                        for k in range(4):
                            ins = A.activation(xT[u % 2][:, 4 * g + k, 0:Ru], b[:, k * Ru:(k + 1) * Ru], ACT.Copy, scale=colw[:, 4 * g + k:4 * g + k + 1])
                        release(ins, ("xT", u, g))
                    released(act, ("xT", u, 1))
                    A.activation(tinya[0:1, 0:1], tinya[0:1, 1:2], ACT.Copy).then_inc(xT_ready, 1)

                if t == 0:
                    act.wait_ge(consts_in, 32)
                    A.activation(tinya[0:1, 0:4], main[0:1, 0:4], ACT.Copy).then_inc(act_chain, 1)
                    act.wait_ge(act_chain, 1)
                    scale_turned(0)
                if t < SAMPLE:
                    scale_turned(t + 1)
                act.wait_ge(x_scaled, t + 1)
                if t >= 2:
                    act.wait_ge(h_stored[t % 2], 64 * (t // 2))
                for n in range(7):
                    w = min(512, INW - 512 * n)
                    b = filled(act, ("proj", t, n))
                    release(A.activation(H[t % 2][0:R, 512 * n:512 * n + w], b[0:R, 0:w], ACT.Copy, scale=tiny[0:R, t % 2:t % 2 + 1]), ("proj", t, n))
                released(act, ("proj", t, 6))
                A.activation(tinya[0:1, 0:1], tinya[0:1, 1:2], ACT.Copy).then_inc(h_ready, 1)
                for u in ([t - 1] if t else []) + ([t] if t == SAMPLE else []):
                    Ru = rows(u)
                    b = filled(act, ("keysT", u))
                    if u < TILES:
                        A.activation(kT[:, u * P:(u + 1) * P], b[:, 0:P], ACT.Copy)
                        ins = A.activation(kiT[:, u * P:(u + 1) * P], b[:, 128:256], ACT.Copy)
                    else:
                        A.activation(knew[:, 0, :], b[:, 0:Ru], ACT.Copy)
                        ins = A.activation(knew[:, 1, :], b[:, 128:128 + Ru], ACT.Copy)
                    release(ins, ("keysT", u))
                    released(act, ("keysT", u))
                    A.activation(tinya[0:1, 0:1], tinya[0:1, 1:2], ACT.Copy).then_inc(keys_kept, 1)

            def note(name, s):
                released(act, name)
                A.activation(tinya[0:1, 0:1], tinya[0:1, 1:2], ACT.Copy).then_inc(s, 1)

            def heads(t):
                if t == 0:
                    act.wait_ge(h_in, 16)
                for name, dst, s in (("qiT", qiT, qi_ready), ("qaT", qaT, qa_ready), ("qrT", qrT, qr_ready), ("krT", krT, kr_ready)):
                    b = filled(act, (name, t))
                    release(A.activation(dst[:].rearrange("p g n -> p (g n)"), b[:, :], ACT.Copy), (name, t))
                    note((name, t), s)
                silu(t)

            def silu(t):
                R = rows(t)
                if t < TILES:
                    filled(act, ("state", t))
                else:
                    act.wait_ge(kd_ready, t + 1)
                act.wait_ge(h_in, 16 * (t + 1))
                A.activation(Hb[0:R, KR:KR + 512], Hb[0:R, GR:GR + 512], ACT.Exp, scale=-1.0).then_inc(exp_g, 1)

            def scores(t):
                for c in range((t + 4) // 4):
                    w = min(512, (t + 1) * P - 512 * c)
                    for h in range(HI):
                        m = score_no[(t, c, h)]
                        b = filled(act, ("score", t, c, h))
                        if m >= 2:
                            act.wait_ge(relu_used, m - 1)
                        release(A.activation(mid[:, m % 2, 0:w], b[:, 0:w], ACT.Relu), ("score", t, c, h))
                        note(("score", t, c, h), relu_ready)

            def attend(t):
                nch = (t + 4) // 4
                L = (t + 1) * P
                for h in range(HA + 1):
                    if h < HA:
                        act.wait_ge(logits_ready, 8 * t + h + 1)
                        s_h = S[:, 1024 * (h % 2):1024 * (h % 2) + L]
                        A.activation(s_h, s_h, ACT.Exp, bias=nmx[:, h:h + 1], scale=HD ** -0.5, accum_out=rs[:, h:h + 1]).then_inc(probs_ready, 1)
                    if h:
                        g = h - 1
                        for c in range(nch):
                            n = min(4, t + 1 - 4 * c)
                            m = turned_no[(t, g, c)]
                            b = filled(act, ("pT", t, g, c))
                            if m - 2 >= turned_no[(t, 0, 0)]:
                                act.wait_ge(pT_used, m - 1 - t)
                            release(A.activation(mid[:, m % 2, 0:n * P], b[:, 0:n * P], ACT.Copy), ("pT", t, g, c))
                            note(("pT", t, g, c), pT_ready)

            def output(t):
                R = rows(t)
                mixT = spare[:, 0:1024].rearrange("p (k n) -> p k n", k=KC)
                nT = spare[:, 1024:2048].rearrange("p (k n) -> p k n", k=KC)
                b = filled(act, ("mixT", t, 0))
                src = b[:, 0:4 * R].rearrange("p (k n) -> p k n", k=4)
                release(A.activation(mixT[:, 0:4, 0:R], src, ACT.Copy), ("mixT", t, 0))
                b = filled(act, ("mixT", t, 1))
                for k in range(4):
                    ins = A.activation(mixT[:, 4 + k, 0:R], b[:, k * R:(k + 1) * R], ACT.Copy, scale=colw[:, 8 + k:9 + k])
                release(ins, ("mixT", t, 1))
                note(("mixT", t, 1), mixT_ready)
                for name, dst, s in (("nT", nT, nT_ready), ("peerq", mixT, peerq_ready)):
                    for g in range(2):
                        b = filled(act, (name, t, g))
                        release(A.activation(dst[:, 4 * g:4 * g + 4, 0:R], b[:, 0:4 * R].rearrange("p (k n) -> p k n", k=4), ACT.Copy), (name, t, g))
                    note((name, t, 1), s)
                for n in range(4):
                    b = filled(act, ("keys", t, n))
                    release(A.activation(Hb[0:R, 512 * n:512 * (n + 1)], b[0:R, :], ACT.Copy), ("keys", t, n))
                note(("keys", t, 3), keys_ready)

            def choose(t):
                R = rows(t)
                act.wait_ge(gate_shifted, t + 1)
                g = gate[0:R, t % 2]
                A.activation(g, g, ACT.Exp).then_inc(gate_exp, 1)

            def peer(t, head):
                R = rows(t)
                with act.Fori(0, 2) as i:
                    for j in range(2):
                        act.wait_ge(hval_ready, i * 2 + (4 * head + j + 1))
                        A.activation(gl[0:R, 4 * j:4 * j + 4], hv[0:R, 4 * j:4 * j + 4], ACT.Gelu).then_inc(gelu_ready, 1)
                        act.wait_ge(coef_ready, i * 2 + (4 * head + j + 1))
                        for s in range(4 * j, 4 * j + 4):
                            act.wait_ge(row_used, i * 8 + (16 * head + s + 1 + RING - 4))
                            A.activation(diag[0:R, s % 4, :], ident[0:R, :], ACT.Copy, scale=coef[0:R, s:s + 1]).then_inc(diag_ready, 1)

            def sheads(t):
                b = filled(act, ("qiT", t))
                release(A.activation(qiS.rearrange("p b h t -> p h b t"), b[0:HD, 0:256].rearrange("p (h b t) -> p h b t", h=HI, b=NB), ACT.Copy), ("qiT", t))
                note(("qiT", t), qi_ready)
                b = filled(act, ("qaT", t))
                release(A.activation(qaS.rearrange("p b h t -> p h b t"), b[:, 0:256].rearrange("p (h b t) -> p h b t", h=HI, b=NB), ACT.Copy), ("qaT", t))
                note(("qaT", t), qa_ready)
                for name, dst, s in (("qrT", spare[:, 512:640], qr_ready), ("krT", spare[:, 640:768], kr_ready)):
                    b = filled(act, (name, t))
                    release(A.activation(dst, b[:, 0:128], ACT.Copy), (name, t))
                    note((name, t), s)
                b = filled(act, ("wiT", t))
                release(A.activation(wiS, b[0:NS, 0:256], ACT.Copy), ("wiT", t))
                note(("wiT", t), wiS_ready)
                silu(t)

            def sscores():
                for b_ in range(NB):
                    for c in range(5):
                        w = 512 if c < 4 else NS
                        if c < 4:
                            b = filled(act, ("skT", b_, c))
                            release(A.activation(mid[0:HD, 0, :], b[0:HD, :], ACT.Copy), ("skT", b_, c))
                            note(("skT", b_, c), skT_ready)
                        b = filled(act, ("sdot", b_, c))
                        release(A.activation(mid[0:NS, 1, 0:w], b[0:NS, 0:w], ACT.Relu), ("sdot", b_, c))
                        note(("sdot", b_, c), srelu_ready)

            def sattend():
                pTs = Hb[:, 768:2816].rearrange("p (k n) -> p k n", k=BLK)
                for g in range(2):
                    for bb in range(4):
                        b_ = 4 * g + bb
                        p0 = 32 * bb
                        for c in range(5):
                            w = 512 if c < 4 else NS
                            if c < 4:
                                b = filled(act, ("sKT", b_, c))
                                release(A.activation(mid[:, c % 2, :], b[:, :], ACT.Copy), ("sKT", b_, c))
                                note(("sKT", b_, c), skT_ready)
                            b = filled(act, ("slog", b_, c))
                            release(A.activation(S[p0:p0 + 32, 512 * c:512 * c + w], b[p0:p0 + 32, 0:w], ACT.Copy), ("slog", b_, c))
                            note(("slog", b_, c), slog_ready)
                    act.wait_ge(smax_ready, g + 1)
                    A.activation(S[:, 0:SL], S[:, 0:SL], ACT.Exp, bias=nmx[:, g:g + 1], scale=HD ** -0.5, accum_out=rs[:, g:g + 1]).then_inc(sexp_ready, 1)
                    for c in range(5):
                        b = filled(act, ("spT", g, c))
                        if c < 4:
                            ins = A.activation(pTs[:, 4 * c:4 * c + 4, :], b[:, :].rearrange("p (k n) -> p k n", k=4), ACT.Copy)
                        else:
                            ins = A.activation(wiS[:, 0:P], b[0:NS, 0:P], ACT.Copy)
                        release(ins, ("spT", g, c))
                    note(("spT", g, 4), spT_ready)

            steps = {"project": project, "heads": heads, "scores": scores, "attend": attend, "output": output,
                     "choose": choose, "sheads": sheads}
            for what, n in schedule:
                if what == "peer":
                    peer(n // 8, n)
                elif what == "sscores":
                    sscores()
                elif what == "sattend":
                    sattend()
                elif what in steps:
                    steps[what](n)

        @block.gpsimd
        def _(pool):
            table_ik = cache_ik.rearrange("(r k) d -> r (k d)", k=BLK)
            table_k = cache_k.rearrange("(r k) d -> r (k d)", k=BLK)
            table_v = cache_v.rearrange("(r k) d -> r (k d)", k=BLK)

            def gather(dst, table, ids, s):
                pool.indirect_dma_start(dst, None, table, bass.IndirectOffsetOnAxis(ap=ids, axis=0)).then_inc(s, 16)

            def peer(t, head, n):
                R = rows(t)
                h = head % PH
                ids = eid[:].rearrange("p a n -> p (a n)")
                pool.wait_ge(chosen, t + 1)
                with pool.Fori(0, n) as i:
                    for k in range(2):
                        nc.gpsimd.tensor_copy(idx8[0:R, k, :], ids[0:R, bass.ds(i * PK + ((t % 2) * SLOTS + h * PK + 8 * k), 8)]).then_inc(idx_ready, 1)
                        pool.wait_ge(idx_ready, i * 2 + (2 * head + k + 1))
                        for s in range(8):
                            pool.wait_ge(row_used, i * 16 + (16 * head + 8 * k + s + 1))
                            pool.sem_inc(slot_granted, 1)
                            gather(ring[0:R, s, :], uv, idx8[0:R, k, s:s + 1], row_in[s])

            gathers = [(what, n, 1) for what, n in schedule if what in ("peer", "sscores", "sattend")]
            runs = []
            for what, n, _ in gathers:
                last = runs[-1] if runs else None
                if what == "peer" and last and last[0] == "peer" and last[1] // 8 == n // 8:
                    last[2] += 1
                else:
                    runs.append([what, n, 1])
            for what, n, count in runs:
                if what == "peer":
                    if n == 0:
                        pool.wait_ge(rotated, TILES + 1)
                        pool.wait_ge(h_ready, TILES + 1)
                    peer(n // 8, n, count)
                elif what == "sscores":
                    pool.wait_ge(gi_ready, 1)
                    pool.wait_ge(states_out, 16)
                    for b in range(NB):
                        if b:
                            filled(pool, ("skT", b - 1, 3))
                        gather(G[:, 0:1024], table_ik, gi[:, b:b + 1], g_in)
                elif what == "sattend":
                    for g in range(2):
                        for table in (table_k, table_v):
                            for bb in range(4):
                                if table is table_k:
                                    if bb:
                                        filled(pool, ("sKT", 4 * g + bb - 1, 3))
                                    elif g:
                                        pool.wait_ge(g_used, 4)
                                    else:
                                        filled(pool, ("skT", NB - 1, 3))
                                elif bb:
                                    pool.wait_ge(g_used, 4 * g + bb)
                                else:
                                    filled(pool, ("sKT", 4 * g + 3, 3))
                                gather(G[:, :], table, gi[:, 4 * g + bb:4 * g + bb + 1], g_in)


_NAMES = ["x_p", "x_s", "cache_k", "cache_v", "cache_ik", "state_in", "pages", "w_in", "w_out", "w_q", "sk", "uv",
          "cols", "wffn", "wfin", "c_rope", "c_main", "c_dec", "c_s32", "c_s128"]
_OUTS = [("y_p", (SEQ, D)), ("y_s", (NS, D)), ("k_p", (SEQ, 128)), ("v_p", (SEQ, 128)), ("ik_p", (SEQ, 64)),
         ("st_p", (P, HR * RD)), ("k_s", (NS, 128)), ("v_s", (NS, 128)), ("ik_s", (NS, 64)), ("st_s", (P, NB, HR, RD))]


def kernel(x_prompt, x_sample, cache_k, cache_v, cache_idx_k, state_ret, page_table,
           norm_attn_w, w_in, ret_gn_w, w_out, norm_ffn_w, peer_w_q,
           peer_sub_keys_1, peer_sub_keys_2, peer_u, peer_v, final_norm_w):
    import numpy as _np
    import concourse.bacc as _bacc
    from concourse import mybir as _mybir
    from concourse.bass_utils import run_bass_kernel_spmd as _run

    a = _np.asarray
    heads = _np.arange(HA * HD).reshape(KVH, HA // KVH, HD).transpose(1, 0, 2).ravel()
    order_in = _np.concatenate([heads, _np.arange(512, INW)])
    order_out = _np.concatenate([heads, _np.arange(512, D)])
    rope, main, dec, s32, s128 = constants()
    sk = _np.zeros((P, 256), _np.float32)
    sk[0:64, 0:128] = a(peer_sub_keys_1)[0].T
    sk[64:128, 128:256] = a(peer_sub_keys_2)[0].T
    arrays = {
        "x_p": a(x_prompt)[0], "x_s": a(x_sample).reshape(NS, D),
        "cache_k": a(cache_k).reshape(-1, 128), "cache_v": a(cache_v).reshape(-1, 128),
        "cache_ik": a(cache_idx_k).reshape(-1, 64),
        "state_in": a(state_ret)[0].transpose(2, 0, 1, 3),
        "pages": _np.repeat(a(page_table).T, 8, axis=0),
        "w_in": a(w_in)[0][:, order_in], "w_out": a(w_out)[0][order_out], "w_q": a(peer_w_q)[0], "sk": sk,
        "uv": _np.concatenate([a(peer_u)[0], a(peer_v)[0]], axis=1),
        "cols": _np.concatenate([a(norm_attn_w).reshape(8, P).T, a(ret_gn_w).reshape(4, P).T], axis=1),
        "wffn": a(norm_ffn_w)[0], "wfin": a(final_norm_w),
        "c_rope": rope, "c_main": main, "c_dec": dec, "c_s32": s32, "c_s128": s128,
    }
    nc = _bacc.Bacc("TRN2", target_bir_lowering=False, num_devices=1)
    feed, args = {}, []
    for name in _NAMES:
        v = _np.ascontiguousarray(arrays[name])
        feed[f"in_{name}"] = v
        args.append(nc.dram_tensor(f"in_{name}", v.shape, _mybir.dt.from_np(v.dtype), kind="ExternalInput").ap())
    for name, shape in _OUTS:
        args.append(nc.dram_tensor(f"out_{name}", shape, F32, kind="ExternalOutput").ap())
    build(nc, *args)
    r = _run(nc, [feed], core_ids=[0]).results[0]
    y_p, y_s, k_p, v_p, ik_p, st_p, k_s, v_s, ik_s, st_s = (a(r[f"out_{n}"]) for n, _ in _OUTS)
    return (y_p.reshape(1, SEQ, D), y_s.reshape(NB, NT, D),
            k_p.reshape(1, 1, SEQ, KVH, HD), v_p.reshape(1, 1, SEQ, KVH, HD), ik_p.reshape(1, 1, SEQ, HD),
            st_p.reshape(P, HR, RD).transpose(1, 0, 2)[None, None],
            k_s.reshape(1, NB, NT, KVH, HD), v_s.reshape(1, NB, NT, KVH, HD), ik_s.reshape(1, NB, NT, HD),
            st_s.transpose(1, 2, 0, 3)[None])
```

```python
from contextlib import ExitStack, nullcontext

import numpy as np

import concourse.bass as bass
from concourse import mybir

F32 = mybir.dt.float32
I32 = mybir.dt.int32
U32 = mybir.dt.uint32
ALU = mybir.AluOpType
ACT = mybir.ActivationFunctionType
AX = mybir.AxisListType

P = 128
D = 1024
KC = D // P
SEQ = 1024
NB, NT = 8, 4
NS = NB * NT
PAST = 2048
PAGE = 128
TILES = SEQ // P
SAMPLE = TILES
HA, HD, KVH = 8, 64, 2
HI = 8
HR, RD = 4, 128
QA, KA, VA, QI, KI, WI, QR, KR, VR, GR = 0, 512, 640, 768, 1280, 1344, 1352, 1864, 2376, 2888
INW = 3400
TOPK = 256
ROUNDS = TOPK // 8
PARTS = 8
PH, PK, NKEY, EXPERTS = 8, 16, 128, 128 * 128
SLOTS = PH * PK
RING = 8
GROUPS = ((0, 1), (1, 3), (3, 5), (5, 8))
EPS = 1e-6
BIG = 1.0e30
OUTSIDE = -3.0e38
CHOSEN = -3.4e38
BLK = 16
SL = PAST + NS
LOGG = [float(np.log1p(-(2.0 ** (-5.0 - h)))) for h in range(HR)]


def constants():
    f = np.float32
    pos = np.concatenate([np.arange(SEQ), PAST + np.tile(np.arange(NT), NB)]).astype(f)

    def table(half, theta):
        ang = pos[:, None] * (f(1.0) / (f(theta) ** (np.arange(half, dtype=f) / f(half)))).astype(f)[None, :]
        return np.cos(ang), np.sin(ang)

    ca, sa = table(8, 500000.0)
    cr, sr = table(64, 10000.0)
    rope = np.concatenate([ca, sa, cr, sr], 1).astype(f)

    def decay(n, same):
        i = np.arange(n)
        lg = np.array(LOGG)
        c = NT if same else n
        within = i % c
        diff = within[None, :] - within[:, None]
        ok = (diff >= 0) & ((i[:, None] // c) == (i[None, :] // c))
        mask = np.where(ok[:, None, :], np.exp(lg[None, :, None] * np.maximum(diff, 0)[:, None, :]), 0) * RD ** -0.5
        qd = np.broadcast_to(np.exp(lg[:, None] * (within[None, :] + 1))[None], (P, HR, n))
        kd = np.exp(lg[None, :] * (c - 1 - within[:, None])) * RD ** -0.5
        return mask.astype(f), qd.astype(f), kd.astype(f)

    md, qd, kd = decay(P, False)
    ms, qs, ks = decay(NS, True)
    main = np.zeros((P, 280), f)
    main[:, 0:128] = np.eye(P)
    main[:, 128:144] = np.arange(16)
    main[:, 144:272] = np.where(np.arange(P)[None, :] <= np.arange(P)[:, None], 0, OUTSIDE)
    main[:, 272:276] = kd
    main[:, 276] = np.arange(P) % 8
    main[:, 277] = np.arange(P) < HD
    main[:, 278] = np.arange(P) >= HD
    dec = np.concatenate([md.reshape(P, -1), qd.reshape(P, -1)], 1)
    tok = np.arange(NS)
    s32 = np.zeros((NS, 128 + 4 + 8 + NB * NS + NS), f)
    s32[:, 0:128] = ms.reshape(NS, -1)
    s32[:, 128:132] = ks
    s32[:, 132:140] = (tok[:, None] // NT) == np.arange(NB)[None, :]
    rep = np.zeros((NS, NB, HA, NT), f)
    for k in range(NS):
        rep[k, k // NT, :, k % NT] = 1
    s32[:, 140:140 + NB * NS] = rep.reshape(NS, -1)
    same = (tok[:, None] // NT == tok[None, :] // NT) & (tok[None, :] <= tok[:, None])
    s32[:, 396:428] = np.where(same, 0, OUTSIDE)
    s128 = np.zeros((P, 128 + NB * NS + 128), f)
    s128[:, 0:128] = qs.reshape(P, -1)
    s128[:, 128:384] = np.broadcast_to(np.eye(NB)[:, :, None], (NB, NB, NT)).reshape(1, -1)
    rows = np.arange(P) % NS // NT
    s128[:, 384:512] = (rows[:, None] // (HA // KVH)) == (np.arange(P)[None, :] // HD)
    quarter = np.arange(P)[:, None] // NS == np.arange(P // NS)[None, :]
    fold = np.concatenate([np.arange(P)[:, None] % NS == np.arange(NS)[None, :], quarter], 1).astype(f)
    return rope, main, dec, s32, s128, fold


def psum_plan(schedule):
    names = []
    for what, t, part in schedule:
        nch = (t + 4) // 4
        if what == "project":
            if t == 0:
                names += [("xT", t, g) for g in range(2)]
            if t < SAMPLE:
                names += [("xT", t + 1, g) for g in range(2)]
            names += [("proj", t, n) for n in range(7)]
            if t:
                names.append(("keysT", t - 1))
            if t == SAMPLE:
                names.append(("keysT", t))
        elif what == "turn":
            names += [(w, t) for w in ("qiT", "qaT", "qrT", "krT")]
        elif what == "retain":
            names += [(w, t) for w in ("decayed", "state")]
        elif what == "scores":
            names += [("score", t, part, h) for h in range(HI)]
        elif what == "attend":
            if part < HA:
                names += [("logit", t, part, c) for c in range(nch)]
            if part:
                names += [("pT", t, part - 1, c) for c in range(nch)]
        elif what == "sheads":
            names += [(w, t) for w in ("qiT", "qrT", "krT", "decayed")]
        elif what == "sstates":
            names += [("sstate", b) for b in range(NB)]
        elif what == "sturn":
            names += [("qaT", t), ("wiT", t)]
        elif what == "sscores":
            b = part
            names += [("skT", b, 0), ("skT", b, 1), ("sdot", b)] if b < NB else [("snew", t), ("snsum", t)]
        elif what == "slogits":
            b = part
            names += [(w, b, c - (w == "slog")) for c in range(6) for w in ("sKT", "slog")
                      if (w == "slog" and c) or (w == "sKT" and c < 4)]
        elif what == "sattend":
            names += [(w, part, c) for w in ("smask", "spT") for c in range(5)]
        elif what == "output":
            names += {0: [("mixT", t, 0), ("mixT", t, 1), ("out", t, 0)], 1: [("out", t, 1)],
                      2: [("nT", t, 0), ("nT", t, 1), ("peerq", t, 0)],
                      3: [("peerq", t, 1)], 4: [("keys", t, n) for n in range(4 if t < TILES else 1)]}[part]
    return {name: (k % 4, k // 4) for k, name in enumerate(names)}


def long_plan(schedule):
    names = []
    for what, t, part in schedule:
        if what in ("retain", "sheads"):
            names.append(("ret", t))
        elif what == "attend" and part == 0:
            names.append(("att", t))
        elif what == "sscores" and part == 0:
            names.append(("ssum", t))
        elif what == "sattend":
            names.append(("satt", part))
    return {name: (k % 2, k // 2) for k, name in enumerate(names)}


def choosing_steps(t):
    w = (t + 1) / TILES
    if t < TILES:
        steps = [(("turn", t, 0), 9)]
        steps += [(("scores", t, c), 9) for c in range((t + 4) // 4) if t >= 2]
        steps += [(("retain", t, 0), 6), (("retained", t, 0), 9)]
        steps += [(("topk", t, k), 9 * w) for k in range(PARTS) if t >= 2]
        steps += [(("mask", t, 0), 1)]
        steps += [(("attend", t, h), 2 + 4.5 * w) for h in range(HA + 1)]
    else:
        steps = [(("sheads", t, 0), 14), (("sstates", t, 0), 26), (("retained", t, 0), 10), (("sturn", t, 0), 8)]
        steps += [(("sscores", t, b), 8) for b in range(NB)] + [(("sscores", t, NB), 10)]
        for k in range(PARTS):
            steps += [(("slogits", t, k // 2), 0)] * (k % 2 == 0) + [(("topk", t, k), 17)]
        steps += [(("mask", t, 0), 2), (("sattend", t, 0), 25), (("svalues", t, 0), 7), (("svalues", t, 1), 4)]
        steps += [(("slogits", t, b), 8) for b in range(4, 8)]
        steps += [(("sattend", t, 1), 20), (("svalues", t, 2), 7), (("svalues", t, 3), 9)]
    steps += [(("output", t, 0), 11), (("output", t, 1), 9), (("norm", t, 0), 6), (("output", t, 2), 10), (("output", t, 3), 8),
              (("output", t, 4), 5)]
    return steps + [(("choose", t, k), w) for k, w in enumerate((8, 9, 7, 7, 7.5, 8) if t < TILES else (3, 4, 2, 2, 2, 3))]


def cache_gathers(step):
    what, _, part = step
    if what == "sscores":
        return 1 if part < NB else 0
    if what == "svalues":
        return 1 if part % 2 else 2
    return 1 if what in ("slogits", "sattend") else 0


def blocks(t):
    return (SLOTS if t < TILES else SLOTS * NS // P) // RING


def heads_of(t):
    return PH if t < TILES else PH * NS // P


def make_schedule():
    s = [("project", t, 0) for t in range(TILES + 1)]
    s += [e for e, _ in choosing_steps(0)]
    for t in range(TILES + 1):
        steps = choosing_steps(t + 1) if t < SAMPLE else []
        total = sum(w for _, w in steps)
        done = 0.0
        for b in range(blocks(t)):
            rows_out = 0
            while steps and done + steps[0][1] / 2 <= total * (b + 1) / blocks(t):
                rows_out += cache_gathers(steps[0][0])
                if rows_out > 2:
                    break
                done += steps[0][1]
                s.append(steps.pop(0)[0])
                if t and s[-1][0] in ("turn", "sheads"):
                    s.append(("finish", t - 1, 0))
            if b == 0:
                s += [("finish", t - 1, 0)] * (t == TILES) + [("seed", t, 0)]
            if b == blocks(t) - 1:
                s += [e for e, _ in steps]
            if s[-1][0] == "peer":
                b0, n = s.pop()[2]
                s.append(("peer", t, (b0, n + 1)))
            else:
                s.append(("peer", t, (b, 1)))
    return s + [("finish", TILES, 0)]


def times(engine, n):
    return engine.Fori(0, n) if n > 1 else nullcontext(0)


def build(nc, x_p, x_s, cache_k, cache_v, cache_ik, state_in, pages, w_in, w_out, w_q, sk, uv,
          cols, wffn, wfin, c_rope, c_main, c_dec, c_s32, c_s128, c_fold,
          y_p, y_s, k_p, v_p, ik_p, st_p, k_s, v_s, ik_s, st_s):
    schedule = make_schedule()
    short, long = psum_plan(schedule), long_plan(schedule)
    score_no = {n[1:]: k for k, n in enumerate(n for n in short if n[0] == "score")}
    turned_no = {n[1:]: k for k, n in enumerate(n for n in short if n[0] == "pT")}

    norm_no = {e: k + 1 for k, e in enumerate(e[0:2] for e in schedule if (e[0], e[2]) in (("output", 0), ("finish", 0)))}

    def rows(t):
        return P if t < TILES else NS

    def x_of(t):
        return x_p[t * P:(t + 1) * P, :] if t < TILES else x_s

    with ExitStack() as ctx:
        def sb(name, shape, dt=F32):
            return ctx.enter_context(nc.sbuf_tensor(name, shape, dt))

        def sem(name):
            return ctx.enter_context(nc.semaphore(name))

        h_dram = nc.dram_tensor("h_scratch", (SEQ + NS, INW), F32, kind="Internal").ap()
        a_dram = nc.dram_tensor("a_scratch", (NB * HA * NT, HD), F32, kind="Internal").ap()

        weights = sb("weights", [P, 128 * 256])
        main = sb("main", [P, 280])
        dec = sb("dec", [P, 1024])
        nw = sb("nw", [P, D])
        keysT = sb("keysT", [P, 256])
        state = sb("state", [P, HR, RD])
        kv = sb("kv", [P, 2048 + SL])
        Hb = sb("Hb", [P, INW])
        spare = sb("spare", [P, 2048 + SL])
        mid = sb("mid", [P, 2, 512])
        h1 = sb("h1", [P, D])
        xn = sb("xn", [P, 2, D])
        eid = sb("eid", [P, 2, SLOTS], I32)
        gate = sb("gate", [P, 2, PH, PK])
        idx8 = sb("idx8", [P, 2, 8], I32)
        diag = sb("diag", [P, 4, P])
        colw = sb("colw", [P, 12])
        tiny = sb("tiny", [P, 64])
        nmx = sb("nmx", [P, 8])
        rs = sb("rs", [P, 8])
        tinya = sb("tinya", [P, 4])
        tinyb = sb("tinyb", [P, 4])
        hv = sb("hv", [P, 8])
        gl = sb("gl", [P, 8])
        coef = sb("coef", [P, 8])

        win = weights[:, 0:KC * INW].rearrange("p (k n) -> p k n", k=KC)
        xa = [weights[:, 27264 + 1024 * i:27264 + 1024 * (i + 1)] for i in range(2)]
        xT = [weights[:, 29312:30336].rearrange("p (k n) -> p k n", k=KC),
              mid[:].rearrange("p a n -> p (a n)").rearrange("p (k n) -> p k n", k=KC)]
        rot = [weights[:, 30336 + 144 * i:30336 + 144 * (i + 1)] for i in range(2)]
        rt = weights[:, 30624:30624 + 2048].rearrange("p (a n) -> p a n", a=4)
        wout_sb = weights[:, 0:8192].rearrange("p (k n) -> p k n", k=KC)
        wq_sb = weights[:, 8192:16384].rearrange("p (k n) -> p k n", k=KC)
        ring = weights[:, 16384:32768].rearrange("p (s n) -> p s n", s=RING)
        ident = main[:, 0:128]
        iota16 = main[:, 128:144]
        causal = main[:, 144:272]
        kT = kv[:, 0:1024]
        kiT = kv[:, 1024:2048]
        vall = kv[:, 2048:3072].rearrange("p (t n) -> p t n", t=TILES)
        sc = kv[:, 3072:4096]
        states = kv[:, 0:NB * 512].rearrange("p (b h e) -> p b h e", b=NB, h=HR)
        G = kv[:, 0:2048]
        gathered = [G, Hb[:, 768:2816]]
        gathered_v = [G, spare[:, 2048:4096]]
        scs = kv[0:NS, 2048:2048 + SL]
        qaT = spare[:, 0:1024].rearrange("p (h n) -> p h n", h=HA)
        qiT = spare[:, 2048:3072].rearrange("p (h n) -> p h n", h=HI)
        qrT, krT = (spare[:, 512 * k:512 * (k + 1)].rearrange("p (g n) -> p g n", g=4) for k in (2, 3))
        H = [Hb, spare[:, 0:INW]]
        S = spare[:, 2048:2048 + SL]
        v16 = spare[:, 1024:1280].rearrange("p (g k) -> p g k", k=PK)
        i16 = spare[:, 1280:1536].bitcast(U32).rearrange("p (g k) -> p g k", k=PK)
        f16 = Hb[:, 2048:2304].rearrange("p (g k) -> p g k", k=PK)
        sv = Hb[:, 2304:2432].rearrange("p (g k) -> p g k", k=PK)
        si = Hb[:, 2432:2560].bitcast(U32).rearrange("p (g k) -> p g k", k=PK)
        ab = Hb[:, 2560:2816].bitcast(U32).rearrange("p (a n) -> p a n", a=2)
        abf = Hb[:, 2816:3072].rearrange("p (a n) -> p a n", a=2)
        pick = Hb[:, 3072:3328].rearrange("p (a n) -> p a n", a=2)
        so = h1[:, 0:256].rearrange("p (g n) -> p g n", g=2)

        s32 = dec[0:NS, 512:512 + 428]
        fold = dec[:, 960:992]
        quarter = dec[:, 992:996]
        s128 = dec[:, 0:512]
        knew = sb("knew", [P, 2, NS])
        pt = sb("pt", [P, NB], I32)
        ptf = sb("ptf", [P, NB])
        gi = sb("gi", [P, NB], I32)
        qiS = spare[:, 0:512].rearrange("p (a b h t) -> p a b h t", a=2, b=NB, h=HA)
        qaS = spare[:, 512:768].rearrange("p (b h t) -> p b h t", b=NB, h=HA)
        qrS = spare[:, 512:640].rearrange("p (h n) -> p h n", h=HR)
        krS = spare[:, 640:768].rearrange("p (h n) -> p h n", h=HR)
        wi_new = spare[:, 768:832]
        wi_past = spare[:, 1024:2048].rearrange("p (b q n) -> p b q n", b=NB, q=P // NS)
        positive = [kv[:, 2048:2560], kv[:, 2560:3072], kv[:, 3072:3136]]
        knewp = spare[0:NS, 896:1024]
        qdm = spare[:, 1024:2048].rearrange("p (b h n) -> p b h n", b=NB, h=HR)
        qpad = S[0:NS, 0:1024].rearrange("p (h c d) -> p h c d", h=HA, c=KVH)

        psum = [ctx.enter_context(nc.psum_tensor(f"bank{i}", [P, 512], F32)) for i in range(6)]
        yacc = ctx.enter_context(nc.psum_tensor("yacc", [P, 1024], F32))
        full = [sem(f"full{i}") for i in range(6)]
        free = [sem(f"free{i}") for i in range(6)]

        def where(name):
            if name in short:
                return short[name]
            b, u = long[name]
            return 4 + b, u

        def bank(name):
            return psum[where(name)[0]]

        def claim(name):
            b, u = where(name)
            if u:
                nc.tensor.wait_ge(free[b], u)
            return psum[b]

        def fill(ins, name):
            ins.then_inc(full[where(name)[0]], 1)

        def filled(eng, name):
            b, u = where(name)
            eng.wait_ge(full[b], u + 1)
            return psum[b]

        def release(ins, name):
            ins.then_inc(free[where(name)[0]], 1)

        def released(eng, name):
            b, u = where(name)
            eng.wait_ge(free[b], u + 1)

        copied = released
        consts_in = sem("consts_in")
        tables_in = sem("tables_in")
        x_in = [sem("x_in0"), sem("x_in1")]
        rot_in = [sem("rot_in0"), sem("rot_in1")]
        win_in = [sem(f"win_in{n}") for n in range(7)]
        weights_in = sem("weights_in")
        x_scaled = sem("x_scaled")
        h_ready = sem("h_ready")
        rotated = sem("rotated")
        h_stored = [sem("h_stored0"), sem("h_stored1")]
        keys_kept = sem("keys_kept")
        h_in = sem("h_in")
        residual_in = sem("residual_in")
        decayed_ready = sem("decayed_ready")
        qd_ready = sem("qd_ready")
        kd_ready = sem("kd_ready")
        state_ready = sem("state_ready")
        relu_used = sem("relu_used")
        mask_ready = sem("mask_ready")
        logits_ready = sem("logits_ready")
        probs_ready = sem("probs_ready")
        pT_used = sem("pT_used")
        silu_ready = sem("silu_ready")
        mix_ready = sem("mix_ready")
        h1_ready = sem("h1_ready")
        xn_ready = sem("xn_ready")
        gate_shifted = sem("gate_shifted")
        gate_exp = sem("gate_exp")
        chosen = sem("chosen")
        packed = sem("packed")
        seeded = sem("seeded")
        row_in = [sem(f"row_in{i}") for i in range(RING)]
        row_used = sem("row_used")
        idx_ready = sem("idx_ready")
        slot_granted = sem("slot_granted")
        hval_ready = sem("hval_ready")
        gelu_ready = sem("gelu_ready")
        coef_ready = sem("coef_ready")
        diag_ready = sem("diag_ready")
        y_scaled = sem("y_scaled")
        norm_in = sem("norm_in")
        sconsts_in = sem("sconsts_in")
        stored = sem("stored")
        dve_chain = sem("dve_chain")
        act_chain = sem("act_chain")
        gated = sem("gated")
        scores_in = sem("scores_in")
        scores_placed = sem("scores_placed")
        states_in = sem("states_in")
        qpad_ready = sem("qpad_ready")
        wi_spread = sem("wi_spread")
        kdm_ready = sem("kdm_ready")
        states_new = sem("states_new")
        states_out = sem("states_out")
        gi_ready = sem("gi_ready")
        g_in = [sem("g_in0"), sem("g_in1")]
        g_used = sem("g_used")
        smax_ready = sem("smax_ready")
        sexp_ready = sem("sexp_ready")
        so_ready = sem("so_ready")
        so_out = sem("so_out")
        att_in = sem("att_in")

        block = ctx.enter_context(nc.Block())
        NSTORE = [0]

        @block.sync
        def _(sp):
            def store(dst, src):
                sp.dma_start(dst, src).then_inc(stored, 16)
                NSTORE[0] += 1

            def load_x(t):
                R = rows(t)
                if t >= 2:
                    b, use = short[("xT", t - 2, 1)]
                    sp.wait_ge(full[b], use + 1)
                    sp.wait_ge(x_scaled, t - 1)
                sp.dma_start(xa[t % 2][0:R, :], x_of(t)).then_inc(x_in[t % 2], 16)

            def load_rot(t):
                if t >= 2:
                    sp.wait_ge(rotated, t - 1)
                sp.dma_start(rot[t % 2][0:rows(t), :], c_rope[t * P:t * P + rows(t), :]).then_inc(rot_in[t % 2], 16)

            sp.dma_start(main[:], c_main).then_inc(consts_in, 16)
            sp.dma_start(colw[:], cols).then_inc(consts_in, 16)
            load_x(0)
            for n in range(7):
                w = min(512, INW - 512 * n)
                sp.dma_start(win[:, :, 512 * n:512 * n + w],
                             w_in[:, 512 * n:512 * n + w].rearrange("(k p) n -> p k n", p=P)).then_inc(win_in[n], 16)
            load_x(1)
            load_rot(0)
            load_rot(1)
            sp.dma_start(dec[:], c_dec).then_inc(tables_in, 16)
            sp.dma_start(keysT[:], sk).then_inc(tables_in, 16)
            sp.dma_start(pt[:], pages).then_inc(tables_in, 16)
            for what, t, part in schedule:
                R = rows(t)
                if what == "project":
                    if t + 2 <= TILES:
                        load_x(t + 2)
                    sp.wait_ge(rotated, t + 1)
                    r0 = t * P
                    sp.dma_start(h_dram[r0:r0 + R, :], H[t % 2][0:R, :]).then_inc(h_stored[t % 2], 16)
                    ko, vo, io = (k_p, v_p, ik_p) if t < TILES else (k_s, v_s, ik_s)
                    o0 = r0 if t < TILES else 0
                    for dst, c0, w in ((ko, KA, 128), (vo, VA, 128), (io, KI, 64)):
                        sp.dma_start(dst[o0:o0 + R, :], H[t % 2][0:R, c0:c0 + w]).then_inc(h_stored[t % 2], 16)
                    if t + 2 <= TILES:
                        load_rot(t + 2)
                elif what in ("turn", "sheads"):
                    sp.wait_ge(h_stored[0], 64 * 5)
                    sp.wait_ge(h_stored[1], 64 * 4)
                    sp.wait_ge(keys_kept, TILES + 1)
                    if t:
                        sp.wait_ge(chosen, t)
                    sp.dma_start(Hb[0:R, :], h_dram[t * P:t * P + R, :]).then_inc(h_in, 16)
                    if t == 0:
                        sp.wait_ge(h_ready, TILES + 1)
                        sp.wait_ge(rotated, TILES + 1)
                        sp.dma_start(wout_sb[:], w_out.rearrange("(k p) n -> p k n", p=P)).then_inc(weights_in, 16)
                        sp.dma_start(wq_sb[:], w_q.rearrange("(k p) n -> p k n", p=P)).then_inc(weights_in, 16)
                    if what == "sheads":
                        sp.wait_ge(qd_ready, TILES)
                        sp.dma_start(s128, c_s128).then_inc(sconsts_in, 16)
                        sp.dma_start(s32, c_s32).then_inc(sconsts_in, 16)
                        sp.dma_start(dec[:, 960:996], c_fold).then_inc(sconsts_in, 16)
                        sp.wait_ge(mix_ready, TILES)
                        sp.dma_start(states[:], state_in).then_inc(states_in, 16)
                elif what == "sstates":
                    sp.wait_ge(states_new, NB)
                    sp.dma_start(st_s, states[:]).then_inc(states_out, 16)
                    sp.dma_start(st_p, state[:].rearrange("p h e -> p (h e)")).then_inc(stored, 16)
                    NSTORE[0] += 1
                elif what == "sscores" and part == NB:
                    copied(sp, ("ssum", t))
                    for q in range(P // NS):
                        sp.dma_start(S[0:NS, 512 * q:512 * (q + 1)], mid[NS * q:NS * (q + 1), 0, :]).then_inc(scores_in, 16)
                elif what == "svalues" and part % 2:
                    g = part // 2
                    sp.wait_ge(so_ready, g + 1)
                    for bb in range(4):
                        for c in range(KVH):
                            r0 = ((4 * g + bb) * HA + 4 * c) * NT
                            p0 = 32 * bb + 16 * c
                            sp.dma_start(a_dram[r0:r0 + 16, :], so[p0:p0 + 16, g, c * HD:(c + 1) * HD]).then_inc(so_out, 16)
                    if g == 0:
                        continue
                    sp.wait_ge(so_out, 16 * 16)
                    for b in range(NB):
                        dst = Hb[4 * b:4 * b + 4, 0:512].rearrange("p (g c d) -> p g c d", c=KVH, d=HD)
                        for c in range(KVH):
                            src = a_dram[b * 32 + 16 * c:b * 32 + 16 * (c + 1), :].rearrange("(g t) d -> t g d", t=NT)
                            sp.dma_start(dst[:, :, c, :], src).then_inc(att_in, 16)
                elif what == "output" and part == 0:
                    if t:
                        sp.wait_ge(seeded, t)
                    if t == SAMPLE:
                        sp.wait_ge(so_out, 16 * 16)
                    sp.dma_start(h1[0:R, :], x_of(t)).then_inc(residual_in, 16)
                    if t >= 2:
                        sp.wait_ge(stored, 16 * NSTORE[0])
                    sp.dma_start(nw[:], wffn.partition_broadcast(P)).then_inc(norm_in, 16)
                elif what == "choose" and part == 0 and t == SAMPLE:
                    sp.wait_ge(xn_ready, t + 1)
                    for q in range(1, P // NS):
                        sp.dma_start(xn[NS * q:NS * (q + 1), t % 2, :], xn[0:NS, t % 2, :]).then_inc(packed, 16)
                elif what == "finish":
                    if t == SAMPLE:
                        sp.wait_ge(stored, 16 * NSTORE[0])
                    else:
                        sp.wait_ge(xn_ready, t + 2)
                    sp.dma_start(nw[:], wfin.partition_broadcast(P)).then_inc(norm_in, 16)
                    sp.wait_ge(y_scaled, t + 1)
                    store(y_p[t * P:t * P + R, :] if t < TILES else y_s, nw[0:R, :])
            sp.wait_ge(stored, 16 * NSTORE[0])
            sp.wait_ge(states_out, 16)

        @block.tensor
        def _(pe):
            pe.sem_inc(row_used, RING)

            def turn_x(t):
                R = rows(t)
                pe.wait_ge(x_in[t % 2], 16 * (t // 2 + 1))
                for g in range(2):
                    b = claim(("xT", t, g))
                    for k in range(4):
                        c = (4 * g + k) * P
                        mm = nc.tensor.transpose(b[:, k * R:(k + 1) * R], xa[t % 2][0:R, c:c + P], ident[0:R, 0:R])
                    fill(mm, ("xT", t, g))

            def turn_keys(t):
                R = rows(t)
                pe.wait_ge(rotated, t + 1)
                b = claim(("keysT", t))
                h = H[t % 2]
                nc.tensor.transpose(b[:, 0:R], h[0:R, KA:KA + 128], ident[0:R, 0:R])
                mm = nc.tensor.transpose(b[:, 128:128 + R], xn[0:R, t % 2, 0:128], ident[0:R, 0:R])
                fill(mm, ("keysT", t))

            def project(t, part):
                R = rows(t)
                if t == 0:
                    pe.wait_ge(consts_in, 32)
                    turn_x(0)
                if t < SAMPLE:
                    turn_x(t + 1)
                copied(pe, ("xT", t, 1))
                for n in range(7):
                    w = min(512, INW - 512 * n)
                    b = claim(("proj", t, n))
                    if t == 0:
                        pe.wait_ge(win_in[n], 16)
                    for k in range(KC):
                        mm = nc.tensor.matmul(b[0:R, 0:w], xT[t % 2][:, k, 0:R], win[:, k, 512 * n:512 * n + w],
                                              start=(k == 0), stop=(k == KC - 1))
                    fill(mm, ("proj", t, n))
                if t:
                    turn_keys(t - 1)
                if t == SAMPLE:
                    turn_keys(t)

            def turn(t, part):
                pe.wait_ge(h_in, 16 * (t + 1))
                for name, c0 in (("qiT", QI), ("qaT", QA), ("qrT", QR), ("krT", KR)):
                    b = claim((name, t))
                    for g in range(4):
                        mm = nc.tensor.transpose(b[:, g * P:(g + 1) * P], Hb[:, c0 + g * P:c0 + (g + 1) * P], ident)
                    fill(mm, (name, t))

            def retain(t, part):
                copied(pe, ("qrT", t))
                copied(pe, ("krT", t))
                b = claim(("decayed", t))
                for h in range(HR):
                    mm = nc.tensor.matmul(b[:, h * P:(h + 1) * P], krT[:, h, :], qrT[:, h, :], start=True, stop=True)
                fill(mm, ("decayed", t))
                pe.wait_ge(qd_ready, t + 1)
                if t:
                    pe.wait_ge(state_ready, t)
                o = claim(("ret", t))
                for h in range(HR):
                    v = Hb[:, VR + h * RD:VR + (h + 1) * RD]
                    nc.tensor.matmul(o[:, h * RD:(h + 1) * RD], krT[:, h, :], v, start=True, stop=False)
                    mm = nc.tensor.matmul(o[:, h * RD:(h + 1) * RD], qrT[:, h, :], state[:, h, :], start=False, stop=True)
                fill(mm, ("ret", t))
                pe.wait_ge(kd_ready, t + 1)
                b = claim(("state", t))
                for h in range(HR):
                    mm = nc.tensor.matmul(b[:, h * RD:(h + 1) * RD], Hb[:, KR + h * RD:KR + (h + 1) * RD],
                                          Hb[:, VR + h * RD:VR + (h + 1) * RD], start=True, stop=True)
                fill(mm, ("state", t))

            def scores(t, c):
                copied(pe, ("qiT", t))
                w = min(512, (t + 1) * P - 512 * c)
                for h in range(HI):
                    b = claim(("score", t, c, h))
                    mm = nc.tensor.matmul(b[:, 0:w], qiT[:, h, :], kiT[:, 512 * c:512 * c + w], start=True, stop=True)
                    fill(mm, ("score", t, c, h))

            def attend(t, h):
                nch = (t + 4) // 4
                if h == 0:
                    copied(pe, ("qaT", t))
                    claim(("att", t))
                o = bank(("att", t))
                if h < HA:
                    for c in range(nch):
                        w = min(512, (t + 1) * P - 512 * c)
                        b = claim(("logit", t, h, c))
                        mm = nc.tensor.matmul(b[:, 0:w], qaT[:, h, :], kT[:, 512 * c:512 * c + w], start=True, stop=True)
                        fill(mm, ("logit", t, h, c))
                if h:
                    g = h - 1
                    pe.wait_ge(probs_ready, 8 * t + g + 1)
                    for c in range(nch):
                        n = min(4, t + 1 - 4 * c)
                        b = claim(("pT", t, g, c))
                        for k in range(n):
                            col = 1024 * (g % 2) + (4 * c + k) * P
                            mm = nc.tensor.transpose(b[:, k * P:(k + 1) * P], S[:, col:col + P], ident)
                        fill(mm, ("pT", t, g, c))
                    for c in range(nch):
                        n = min(4, t + 1 - 4 * c)
                        m = turned_no[(t, g, c)]
                        copied(pe, ("pT", t, g, c))
                        for k in range(n):
                            kt = 4 * c + k
                            mm = nc.tensor.matmul(o[:, g * HD:(g + 1) * HD], mid[:, m % 2, k * P:(k + 1) * P],
                                                  vall[:, kt, HD * (g % 2):HD * (g % 2) + HD],
                                                  start=(kt == 0), stop=(kt == t))
                        if not (c == nch - 1 and g == HA - 1):
                            mm.then_inc(pT_used, 1)
                if h == HA:
                    fill(mm, ("att", t))

            def output(t, part):
                [output_0, output_1, output_2, output_3, output_4][part](t)

            mixT = spare[:, 0:1024].rearrange("p (k n) -> p k n", k=KC)
            nT = spare[:, 1024:2048].rearrange("p (k n) -> p k n", k=KC)

            def out_half(t, n):
                R = rows(t)
                b = claim(("out", t, n))
                for k in range(KC):
                    mm = nc.tensor.matmul(b[0:R, :], mixT[:, k, 0:R], wout_sb[:, k, 512 * n:512 * (n + 1)],
                                          start=(k == 0), stop=(k == KC - 1))
                fill(mm, ("out", t, n))

            def peer_queries(t, g):
                R = rows(t)
                b = claim(("peerq", t, g))
                for h in range(4 * g, 4 * g + 4):
                    for k in range(KC):
                        mm = nc.tensor.matmul(b[:, (h % 4) * R:(h % 4 + 1) * R], wq_sb[:, k, h * P:(h + 1) * P], nT[:, k, 0:R],
                                              start=(k == 0), stop=(k == KC - 1))
                fill(mm, ("peerq", t, g))

            def output_0(t):
                R = rows(t)
                pe.wait_ge(mix_ready, t + 1)
                if t == SAMPLE:
                    pe.wait_ge(att_in, 16 * NB * KVH)
                if t == 0:
                    pe.wait_ge(weights_in, 32)
                for g in range(2):
                    b = claim(("mixT", t, g))
                    for k in range(4):
                        c = (0 if g == 0 else GR) + k * P
                        mm = nc.tensor.transpose(b[:, k * R:(k + 1) * R], Hb[0:R, c:c + P], ident[0:R, 0:R])
                    fill(mm, ("mixT", t, g))
                copied(pe, ("mixT", t, 1))
                out_half(t, 0)

            def output_1(t):
                out_half(t, 1)

            def output_2(t):
                R = rows(t)
                pe.wait_ge(xn_ready, t + 1)
                for g in range(2):
                    b = claim(("nT", t, g))
                    for k in range(4):
                        c = (4 * g + k) * P
                        mm = nc.tensor.transpose(b[:, k * R:(k + 1) * R], xn[0:R, t % 2, c:c + P], ident[0:R, 0:R])
                    fill(mm, ("nT", t, g))
                copied(pe, ("nT", t, 1))
                peer_queries(t, 0)

            def output_3(t):
                peer_queries(t, 1)

            def output_4(t):
                R = rows(t)
                copied(pe, ("peerq", t, 1))
                if t == SAMPLE:
                    b = claim(("keys", t, 0))
                    for h in range(PH):
                        p0 = NS * (h // 2)
                        mm = nc.tensor.matmul(b[p0:p0 + NS, (h % 2) * 256:(h % 2 + 1) * 256], mixT[:, h, 0:NS], keysT[:, :],
                                              start=True, stop=True)
                    fill(mm, ("keys", t, 0))
                    return
                for n in range(4):
                    b = claim(("keys", t, n))
                    for h in (2 * n, 2 * n + 1):
                        mm = nc.tensor.matmul(b[0:R, (h % 2) * 256:(h % 2 + 1) * 256], mixT[:, h, 0:R], keysT[:, :],
                                              start=True, stop=True)
                    fill(mm, ("keys", t, n))

            def seed(t, part):
                R = rows(t)
                pe.wait_ge(h1_ready, t + 1)
                if t:
                    pe.wait_ge(y_scaled, t)
                for j in range(2):
                    mm = nc.tensor.matmul(yacc[:, 512 * j:512 * (j + 1)], ident[0:R, :], h1[0:R, 512 * j:512 * (j + 1)],
                                          start=True, stop=False, skip_group_check=True)
                mm.then_inc(seeded, 1)

            def peer(t, part):
                b0, n = part
                b0 += (SLOTS // RING) * t
                W = P if t < TILES else NS
                with times(pe, n) as i:
                    for s in range(RING):
                        pe.wait_ge(diag_ready, i * RING + (RING * b0 + s + 1))
                        for j in range(2):
                            mm = nc.tensor.matmul(yacc[0:W, 512 * j:512 * (j + 1)], diag[:, s % 4, 0:W],
                                                  ring[:, s, D + 512 * j:D + 512 * (j + 1)],
                                                  start=False, stop=False, skip_group_check=True)
                        mm.then_inc(row_used, 1)

            def sheads(t, part):
                pe.wait_ge(h_in, 16 * (t + 1))
                b = claim(("qiT", t))
                for k in range(9):
                    c = QI + P * k if k < 4 else QI - HD + P * (k - 4)
                    mm = nc.tensor.transpose(b[:, k * NS:(k + 1) * NS], Hb[0:NS, c:c + P], ident[0:NS, 0:NS])
                fill(mm, ("qiT", t))
                for name, c0 in (("qrT", QR), ("krT", KR)):
                    b = claim((name, t))
                    for g in range(4):
                        mm = nc.tensor.transpose(b[:, g * NS:(g + 1) * NS], Hb[0:NS, c0 + g * P:c0 + (g + 1) * P], ident[0:NS, 0:NS])
                    fill(mm, (name, t))
                copied(pe, ("qrT", t))
                copied(pe, ("krT", t))
                b = claim(("decayed", t))
                for h in range(HR):
                    mm = nc.tensor.matmul(b[0:NS, h * NS:(h + 1) * NS], krS[:, h, :], qrS[:, h, :], start=True, stop=True)
                fill(mm, ("decayed", t))
                pe.wait_ge(qd_ready, t + 1)
                pe.wait_ge(states_in, 16)
                o = claim(("ret", t))
                for h in range(HR):
                    oh = o[0:NS, h * RD:(h + 1) * RD]
                    nc.tensor.matmul(oh, S[0:NS, 1280 + h * NS:1280 + (h + 1) * NS], Hb[0:NS, VR + h * RD:VR + (h + 1) * RD],
                                     start=True, stop=False)
                    for k in range(NB):
                        mm = nc.tensor.matmul(oh, qdm[:, k, h, :], states[:, k, h, :], start=False, stop=(k == NB - 1))
                fill(mm, ("ret", t))

            def sstates(t, part):
                for k in range(NB):
                    pe.wait_ge(kdm_ready, k + 1)
                    b = claim(("sstate", k))
                    for h in range(HR):
                        mm = nc.tensor.matmul(b[:, h * RD:(h + 1) * RD], mid[0:NS, k % 2, h * RD:(h + 1) * RD],
                                              Hb[0:NS, VR + h * RD:VR + (h + 1) * RD], start=True, stop=True)
                    fill(mm, ("sstate", k))

            def sturn(t, part):
                pe.wait_ge(qpad_ready, 1)
                b = claim(("qaT", t))
                for h in range(HA):
                    mm = nc.tensor.transpose(b[:, h * NS:(h + 1) * NS], qpad[:, h, :, :].rearrange("p c d -> p (c d)"), ident[0:NS, 0:NS])
                fill(mm, ("qaT", t))
                pe.wait_ge(wi_spread, 1)
                b = claim(("wiT", t))
                for k in range(NB):
                    nc.tensor.transpose(b[:, k * NS:(k + 1) * NS], S[0:NS, P * k:P * (k + 1)], ident[0:NS, 0:NS])
                for g in range(2):
                    mm = nc.tensor.transpose(b[:, 256 + g * NS:256 + (g + 1) * NS], S[0:NS, 1024 + P * g:1024 + P * (g + 1)], ident[0:NS, 0:NS])
                fill(mm, ("wiT", t))

            def sscores(t, b_):
                if b_ < NB:
                    pe.wait_ge(g_in[b_ % 2], 16 * (b_ // 2 + 1))
                    for half in range(2):
                        b = claim(("skT", b_, half))
                        for j in range(4):
                            c = 1024 * (b_ % 2) + (4 * half + j) * P
                            mm = nc.tensor.transpose(b[:, j * P:(j + 1) * P], G[:, c:c + P], ident)
                        fill(mm, ("skT", b_, half))
                if b_ == 0:
                    copied(pe, ("qiT", t))
                    copied(pe, ("wiT", t))
                    claim(("ssum", t))
                else:
                    copied(pe, ("sdot", b_ - 1))
                    mm = nc.tensor.matmul(bank(("ssum", t))[:, :], wi_past[:, b_ - 1, :, :].rearrange("p q n -> p (q n)"),
                                          positive[(b_ - 1) % 2], start=(b_ == 1), stop=(b_ == NB))
                if b_ < NB:
                    copied(pe, ("skT", b_, 1))
                    b = claim(("sdot", b_))
                    for q in range(4):
                        mm = nc.tensor.matmul(b[NS * q:NS * (q + 1), :], qiS[:, q % 2, b_, :, :].rearrange("p h t -> p (h t)"),
                                              mid[:, q // 2, :], start=True, stop=True)
                    fill(mm, ("sdot", b_))
                    return
                fill(mm, ("ssum", t))
                b = claim(("snew", t))
                for g in range(2):
                    mm = nc.tensor.matmul(b[:, NS * g:NS * (g + 1)], qiS[:, 0, 4 * g:4 * g + 4, :, :].rearrange("p b h t -> p (b h t)"),
                                          knew[:, 1, :], start=True, stop=True)
                fill(mm, ("snew", t))
                copied(pe, ("snew", t))
                b = claim(("snsum", t))
                for g in range(2):
                    mm = nc.tensor.matmul(b[0:NS, 0:NS], wi_new[:, NS * g:NS * (g + 1)], positive[2][:, NS * g:NS * (g + 1)],
                                          start=(g == 0), stop=(g == 1))
                fill(mm, ("snsum", t))

            def slogits(t, b_):
                copied(pe, ("qaT", SAMPLE))
                g, bb = b_ // 4, b_ % 4
                pe.wait_ge(g_in[bb % 2], 16 * (4 + 4 * g + bb // 2 + 1))
                Gk = gathered[b_ % 2]
                q = qaS[:, b_, :, :].rearrange("p h t -> p (h t)")
                for c in range(6):
                    if c < 4:
                        b = claim(("sKT", b_, c))
                        for k in range(4):
                            mm = nc.tensor.transpose(b[:, k * P:(k + 1) * P], Gk[:, (4 * c + k) * P:(4 * c + k + 1) * P], ident)
                        fill(mm, ("sKT", b_, c))
                    if c == 0:
                        continue
                    d = c - 1
                    w = 512 if d < 4 else NS
                    if d < 4:
                        copied(pe, ("sKT", b_, d))
                        rhs = mid[:, d % 2, :]
                    else:
                        rhs = knew[:, 0, :]
                    b = claim(("slog", b_, d))
                    mm = nc.tensor.matmul(b[32 * bb:32 * bb + 32, 0:w], q, rhs, start=True, stop=True)
                    fill(mm, ("slog", b_, d))

            def sattend(t, g):
                pe.wait_ge(mask_ready, SAMPLE + 1)
                for c in range(5):
                    b = claim(("smask", g, c))
                    rep = s32[:, 140 + 4 * g * NS:140 + 4 * (g + 1) * NS]
                    if c < 4:
                        neg = scs[:, 0:PAST].rearrange("q (p k) -> q k p", k=BLK)[:, 4 * c:4 * c + 4, :]
                        mm = nc.tensor.matmul(b[:, :].rearrange("q (k p) -> q k p", p=P), rep, neg, start=True, stop=True)
                    else:
                        mm = nc.tensor.matmul(b[:, 0:NS], rep, scs[:, PAST:SL], start=True, stop=True)
                    fill(mm, ("smask", g, c))
                pe.wait_ge(sexp_ready, g + 1)
                pTs = Hb[:, 768:2816].rearrange("p (k n) -> p k n", k=BLK)
                for c in range(5):
                    b = claim(("spT", g, c))
                    if c < 4:
                        for k in range(4):
                            mm = nc.tensor.transpose(b[:, k * P:(k + 1) * P], S[:, (4 * c + k) * P:(4 * c + k + 1) * P], ident)
                    else:
                        mm = nc.tensor.transpose(b[0:NS, 0:P], S[:, PAST:SL], ident)
                    fill(mm, ("spT", g, c))
                copied(pe, ("spT", g, 4))
                claim(("satt", g))
                weigh_values(g, 0)

            def weigh_values(g, bb):
                pTs = Hb[:, 768:2816].rearrange("p (k n) -> p k n", k=BLK)
                pe.wait_ge(g_in[bb % 2], 16 * (4 + 4 * g + 2 + bb // 2 + 1))
                ob = bank(("satt", g))[32 * bb:32 * bb + 32, 0:P]
                for k in range(BLK):
                    mm = nc.tensor.matmul(ob, pTs[:, k, 32 * bb:32 * bb + 32], gathered_v[bb % 2][:, k * P:(k + 1) * P], start=(k == 0), stop=False)
                mm.then_inc(g_used, 1)
                return nc.tensor.matmul(ob, knewp[:, 32 * bb:32 * bb + 32], Hb[0:NS, VA:VA + P], start=False, stop=True)

            def svalues(t, part):
                g = part // 2
                if part % 2 == 0:
                    weigh_values(g, 1)
                    weigh_values(g, 2)
                else:
                    fill(weigh_values(g, 3), ("satt", g))

            steps = {"project": project, "turn": turn, "retain": retain, "scores": scores, "attend": attend,
                     "output": output, "seed": seed, "peer": peer, "sheads": sheads, "sstates": sstates,
                     "sturn": sturn, "sscores": sscores,
                     "slogits": slogits, "sattend": sattend, "svalues": svalues}
            for what, t, part in schedule:
                if what in steps:
                    steps[what](t, part)

        @block.vector
        def _(dve):
            V = nc.vector
            count = [0]

            def link(ins):
                count[0] += 1
                ins.then_inc(dve_chain, 1)
                dve.wait_ge(dve_chain, count[0])

            def tt(o, a, b, op):
                link(V.tensor_tensor(o, a, b, op))

            def inverse_root(dst, src, R, w):
                y, a = tiny[0:R, 58:58 + w], tinyb[0:R, 0:w]
                link(V.tensor_scalar(y.bitcast(I32), src.bitcast(I32), -0.5, float(0x5F3759DF), ALU.mult, ALU.add))
                for k in range(3):
                    tt(a, y, y, ALU.mult)
                    tt(a, a, src, ALU.mult)
                    link(V.tensor_scalar(a, a, -0.5, 1.5, ALU.mult, ALU.add))
                    if k < 2:
                        tt(y, y, a, ALU.mult)
                return V.tensor_tensor(dst, y, a, ALU.mult)

            def inverse_rms(dst, src, R):
                st = tiny[0:R, 8:20]
                for j in range(2):
                    link(V.bn_stats(st[:, 6 * j:6 * j + 6], src[0:R, 512 * j:512 * (j + 1)]))
                link(V.bn_aggr(tiny[0:R, 20:22], st))
                link(V.scalar_tensor_tensor(tiny[0:R, 22:23], tiny[0:R, 20:21], tiny[0:R, 20:21], tiny[0:R, 21:22], ALU.mult, ALU.add))
                link(V.tensor_scalar(tiny[0:R, 22:23], tiny[0:R, 22:23], EPS, None, ALU.add))
                return inverse_root(dst, tiny[0:R, 22:23], R, 1)

            def scale_x(t):
                R = rows(t)
                dve.wait_ge(x_in[t % 2], 16 * (t // 2 + 1))
                inverse_rms(tiny[0:R, t % 2:t % 2 + 1], xa[t % 2], R).then_inc(x_scaled, 1)

            def rotate(h, c0, n, hd, half, cos, sin, R):
                x = h[0:R, c0:c0 + n * hd].rearrange("p (n d) -> p n d", n=n)
                x1, x2 = x[:, :, 0:half], x[:, :, half:2 * half]
                cb = cos[0:R, None, :].broadcast_to((R, n, half))
                sb_ = sin[0:R, None, :].broadcast_to((R, n, half))
                t4 = [rt[0:R, a, 0:n * half].rearrange("p (n d) -> p n d", n=n) for a in range(4)]
                V.tensor_tensor(t4[0], x1, cb, ALU.mult)
                V.tensor_tensor(t4[1], x2, sb_, ALU.mult)
                V.tensor_tensor(t4[2], x2, cb, ALU.mult)
                link(V.tensor_tensor(t4[3], x1, sb_, ALU.mult))
                V.tensor_tensor(x1, t4[0], t4[1], ALU.subtract)
                return V.tensor_tensor(x2, t4[2], t4[3], ALU.add)

            def project(t, part):
                R = rows(t)
                if t == 0:
                    link(V.memset(state[:], 0.0))
                    scale_x(0)
                if t < SAMPLE:
                    scale_x(t + 1)
                dve.wait_ge(h_ready, t + 1)
                dve.wait_ge(rot_in[t % 2], 16 * (t // 2 + 1))
                r, h = rot[t % 2], H[t % 2]
                link(rotate(h, QA, HA + KVH, HD, 8, r[:, 0:8], r[:, 8:16], R))
                link(rotate(h, QI, HI + 1, HD, 8, r[:, 0:8], r[:, 8:16], R))
                link(rotate(h, QR, 2 * HR, RD, 64, r[:, 16:80], r[:, 80:144], R))
                link(V.tensor_scalar(h[0:R, WI:WI + HI], h[0:R, WI:WI + HI], HI ** -0.5 * HD ** -0.5, None, ALU.mult))
                if t < TILES:
                    V.tensor_copy(vall[:, t, :], h[:, VA:VA + 128])
                ki2 = h[0:R, None, KI:KI + HD].broadcast_to((R, 2, HD))
                V.tensor_copy(xn[0:R, t % 2, 0:128].rearrange("p (a d) -> p a d", a=2), ki2).then_inc(rotated, 1)

            def retained(t, part):
                R = rows(t)
                o = filled(dve, ("ret", t))
                for h in range(HR):
                    link(V.bn_stats(tiny[0:R, 8:14], o[0:R, h * RD:(h + 1) * RD]))
                    link(V.bn_aggr(tiny[0:R, 24 + 2 * h:26 + 2 * h], tiny[0:R, 8:14]))
                ms = tiny[0:R, 24:32].rearrange("p (h a) -> p h a", a=2)
                link(V.tensor_scalar(tiny[0:R, 32:36], ms[:, :, 1], EPS, None, ALU.add))
                link(inverse_root(tiny[0:R, 32:36], tiny[0:R, 32:36], R, HR))
                on = Hb[0:R, QR:QR + 512]
                for h in range(HR):
                    ins = V.tensor_scalar(on[:, h * RD:(h + 1) * RD], o[0:R, h * RD:(h + 1) * RD], tiny[0:R, 24 + 2 * h:25 + 2 * h],
                                          tiny[0:R, 32 + h:33 + h], ALU.subtract, ALU.mult)
                    if h < HR - 1:
                        link(ins)
                release(ins, ("ret", t))
                released(dve, ("ret", t))
                g = Hb[0:R, GR:GR + 512]
                dve.wait_ge(silu_ready, t + 1)
                e = Hb[0:R, KR:KR + 512]
                V.tensor_tensor(g, e, on, ALU.mult).then_inc(gated, 1)

            def retain(t, part):
                dve.wait_ge(h_in, 16 * (t + 1))
                dve.wait_ge(tables_in, 48)
                b = filled(dve, ("decayed", t))
                release(V.tensor_tensor(krT[:].rearrange("p g n -> p (g n)"), b[:, :], dec[:, 0:512], ALU.mult), ("decayed", t))
                V.tensor_tensor(qrT[:].rearrange("p g n -> p (g n)"), qrT[:].rearrange("p g n -> p (g n)"),
                                dec[:, 512:1024], ALU.mult).then_inc(qd_ready, 1)
                filled(dve, ("krT", t))
                kr = Hb[:, KR:KR + 512].rearrange("p (h d) -> p h d", h=HR)
                V.tensor_tensor(kr, kr, main[:, 272:276, None].broadcast_to((P, HR, RD)), ALU.mult).then_inc(kd_ready, 1)
                b = filled(dve, ("state", t))
                for h in range(HR):
                    ins = V.scalar_tensor_tensor(state[:, h, :], state[:, h, :], float(np.exp(LOGG[h] * P)),
                                                 b[:, h * RD:(h + 1) * RD], ALU.mult, ALU.add)
                    if h < HR - 1:
                        link(ins)
                release(ins, ("state", t))
                released(dve, ("state", t))
                V.memset(tiny[0:1, 37:38], 0.0).then_inc(state_ready, 1)

            def scores(t, c):
                w = min(512, (t + 1) * P - 512 * c)
                for h in range(HI):
                    m = score_no[(t, c, h)]
                    copied(dve, ("score", t, c, h))
                    d = sc[:, 512 * c:512 * c + w]
                    wi = Hb[:, WI + h:WI + h + 1]
                    if h == 0:
                        V.tensor_scalar(d, mid[:, m % 2, 0:w], wi, None, ALU.mult).then_inc(relu_used, 1)
                    else:
                        V.scalar_tensor_tensor(d, mid[:, m % 2, 0:w], wi, d, ALU.mult, ALU.add).then_inc(relu_used, 1)
                    dve.wait_ge(relu_used, m + 1)
                if c == t // 4:
                    tt(sc[:, t * P:(t + 1) * P], sc[:, t * P:(t + 1) * P], causal, ALU.add)

            def topk(t, part):
                a = sc[:, 0:(t + 1) * P] if t < TILES else scs
                R = rows(t)
                if t == SAMPLE and part == 0:
                    tt(scs[:, PAST:SL], scs[:, PAST:SL], s32[:, 396:428], ALU.add)
                for _ in range(ROUNDS // PARTS):
                    link(V.max(tiny[0:R, 40:48], a))
                    link(V.match_replace(a, tiny[0:R, 40:48], a, CHOSEN))

            def mask(t, part):
                if t < 2:
                    if t:
                        link(V.memset(sc[:, 0:t * P], 0.0))
                    V.tensor_scalar(sc[:, t * P:(t + 1) * P], causal, -1.0, -BIG, ALU.is_lt, ALU.mult).then_inc(mask_ready, 1)
                else:
                    a = sc[:, 0:(t + 1) * P] if t < TILES else scs
                    V.tensor_scalar(a, a, -3.3e38, -BIG, ALU.is_gt, ALU.mult).then_inc(mask_ready, 1)
                dve.wait_ge(mask_ready, t + 1)

            def attend(t, h):
                nch = (t + 4) // 4
                if h < HA:
                    if h >= 2:
                        filled(dve, ("pT", t, h - 2, nch - 1))
                    for c in range(nch):
                        w = min(512, (t + 1) * P - 512 * c)
                        b = filled(dve, ("logit", t, h, c))
                        ins = V.tensor_tensor_reduce(S[:, 1024 * (h % 2) + 512 * c:1024 * (h % 2) + 512 * c + w], b[:, 0:w],
                                                     sc[:, 512 * c:512 * c + w], 1.0, -3.0e38, ALU.add, ALU.max,
                                                     tiny[:, 48 + c:49 + c])
                        release(ins, ("logit", t, h, c))
                    released(dve, ("logit", t, h, nch - 1))
                    if nch == 2:
                        V.tensor_scalar(nmx[:, h:h + 1], tiny[:, 48:49], tiny[:, 49:50], -HD ** -0.5, ALU.max, ALU.mult).then_inc(logits_ready, 1)
                    else:
                        V.tensor_scalar(nmx[:, h:h + 1], tiny[:, 48:49], -HD ** -0.5, None, ALU.mult).then_inc(logits_ready, 1)
                    dve.wait_ge(logits_ready, 8 * t + h + 1)
                    return
                dve.wait_ge(probs_ready, 8 * (t + 1))
                link(V.reciprocal(tiny[:, 50:58], rs[:, 0:8]))
                o = filled(dve, ("att", t))
                dst = Hb[:, 0:512].rearrange("p (h d) -> p h d", h=HA)
                release(V.tensor_tensor(dst, o[:, :].rearrange("p (h d) -> p h d", h=HA),
                                        tiny[:, 50:58, None].broadcast_to((P, HA, HD)), ALU.mult), ("att", t))
                released(dve, ("att", t))
                V.memset(tiny[0:1, 36:37], 0.0).then_inc(mix_ready, 1)

            def output(t, part):
                R = rows(t)
                if part < 2:
                    n = part
                    dve.wait_ge(residual_in, 16 * (t + 1))
                    b = filled(dve, ("out", t, n))
                    release(V.tensor_tensor(h1[0:R, 512 * n:512 * (n + 1)], b[0:R, :], h1[0:R, 512 * n:512 * (n + 1)], ALU.add), ("out", t, n))
                    released(dve, ("out", t, n))

            def norm(t, part):
                R = rows(t)
                inverse_rms(tiny[0:R, 2:3], h1, R).then_inc(h1_ready, 1)
                dve.wait_ge(h1_ready, t + 1)
                dve.wait_ge(norm_in, 16 * norm_no[("output", t)])
                V.scalar_tensor_tensor(xn[0:R, t % 2, :], h1[0:R, :], tiny[0:R, 2:3], nw[0:R, :], ALU.mult, ALU.mult).then_inc(xn_ready, 1)
                dve.wait_ge(xn_ready, t + 1)

            def top16(groups):
                last = [0] * len(groups)
                for step in range(5):
                    for k, (vals, idxs, a) in enumerate(groups):
                        if step:
                            dve.wait_ge(dve_chain, last[k])
                        half = slice(0, 8) if step < 3 else slice(8, 16)
                        if step in (0, 3):
                            ins = V.max(vals[:, half], a)
                        elif step == 2:
                            ins = V.match_replace(a, vals[:, half], a, CHOSEN)
                        else:
                            ins = V.max_index(idxs[:, half], vals[:, half], a)
                        ins.then_inc(dve_chain, 1)
                        count[0] += 1
                        last[k] = count[0]
                dve.wait_ge(dve_chain, count[0])

            def choose(t, part):
                nh = heads_of(t)
                [choose_0, choose_1, choose_2, choose_2, choose_4, choose_5][part](t, part, nh, nh * PK)

            def top_keys(t, groups):
                copied(dve, ("keys", t, 3 if t < TILES else 0))
                for g0 in range(groups.start, groups.stop, 2):
                    top16([(v16[:, g, :], i16[:, g, :], Hb[:, NKEY * g:NKEY * (g + 1)]) for g in (g0, g0 + 1)])

            def choose_0(t, part, nh, n):
                top_keys(t, range(nh))

            def choose_1(t, part, nh, n):
                top_keys(t, range(nh, 2 * nh))
                link(V.tensor_copy(f16[:, 0:2 * nh], i16[:, 0:2 * nh]))
                cand = S[:, 0:n * PK].rearrange("p (h i j) -> p h i j", h=nh, i=PK)
                v4 = v16[:, 0:2 * nh].rearrange("p (h a) k -> p h a k", a=2)
                tt(cand, v4[:, :, 0, :, None].broadcast_to((P, nh, PK, PK)), v4[:, :, 1, None, :].broadcast_to((P, nh, PK, PK)), ALU.add)

            def choose_2(t, part, nh, n):
                top16([(sv[:, h, :], si[:, h, :], S[:, 256 * h:256 * (h + 1)])
                       for h in range((part - 2) * nh // 2, (part - 1) * nh // 2)])
                if part == 3:
                    V.tensor_tensor(gate[:, t % 2, 0:nh], sv[:, 0:nh], sv[:, 0:nh, 0:1].broadcast_to((P, nh, PK)),
                                    ALU.subtract).then_inc(gate_shifted, 1)

            def choose_4(t, part, nh, n):
                siv = si[:].rearrange("p h k -> p (h k)")
                link(V.tensor_scalar(ab[:, 0, 0:n], siv[:, 0:n], 4, None, ALU.logical_shift_right))
                link(V.tensor_scalar(ab[:, 1, 0:n], siv[:, 0:n], 15, None, ALU.bitwise_and))
                link(V.tensor_copy(abf[:, :, 0:n], ab[:, :, 0:n]))
                look_up(t, 0, nh, n)

            def look_up(t, a, nh, n):
                f4 = f16[:, 0:2 * nh].rearrange("p (h a) k -> p h a k", a=2)
                eq = Hb[:, 0:n * PK].rearrange("p (n i) -> p n i", i=PK)
                eq4 = Hb[:, 0:n * PK].rearrange("p (h k i) -> p h k i", h=nh, i=PK)
                tt(eq, abf[:, a, 0:n, None].broadcast_to((P, n, PK)), iota16[:, None, :].broadcast_to((P, n, PK)), ALU.is_equal)
                tt(eq4, eq4, f4[:, :, a, None, :].broadcast_to((P, nh, PK, PK)), ALU.mult)
                link(V.tensor_reduce(pick[:, a, 0:n], eq, AX.X, ALU.add))

            def choose_5(t, part, nh, n):
                g = gate[:, t % 2, 0:nh]
                look_up(t, 1, nh, n)
                link(V.scalar_tensor_tensor(abf[:, 0, 0:n], pick[:, 0, 0:n], float(NKEY), pick[:, 1, 0:n], ALU.mult, ALU.add))
                link(V.tensor_copy(eid[:, t % 2, 0:n], abf[:, 0, 0:n]))
                dve.wait_ge(gate_exp, t + 1)
                total = tiny[:, 50:50 + nh]
                link(V.tensor_reduce(total, g, AX.X, ALU.add))
                link(V.reciprocal(total, total))
                V.tensor_tensor(g, g, total[:, :, None].broadcast_to((P, nh, PK)), ALU.mult).then_inc(chosen, 1)
                dve.wait_ge(chosen, t + 1)

            def peer(t, part):
                b, n = part
                b0 = (SLOTS // RING) * t + b
                gates = gate[:].rearrange("p a h k -> p (a h k)")
                if t == SAMPLE and b == 0:
                    dve.wait_ge(packed, 16 * 3)
                with times(dve, n) as i:
                    for j, (s0, s1) in enumerate(GROUPS):
                        for s in range(s0, s1):
                            dve.wait_ge(row_in[s], i * 16 + 16 * (b0 + 1))
                            u = ring[:, s, 0:D]
                            ins = V.tensor_tensor_reduce(u, u, xn[:, t % 2, :], 1.0, 0.0, ALU.mult, ALU.add, hv[:, s:s + 1])
                        ins.then_inc(hval_ready, 1)
                        dve.wait_ge(gelu_ready, i * len(GROUPS) + (len(GROUPS) * b0 + j + 1))
                        col = (t % 2) * SLOTS + RING * b + s0
                        V.tensor_tensor(coef[:, s0:s1], gl[:, s0:s1],
                                        gates[:, bass.ds(i * RING + col, s1 - s0)], ALU.mult).then_inc(coef_ready, 1)

            def finish(t, part):
                R = rows(t)
                dve.wait_ge(row_used, RING + SLOTS * t + RING * blocks(t))
                link(inverse_rms(tiny[0:R, 3:4], yacc, R))
                dve.wait_ge(norm_in, 16 * norm_no[("finish", t)])
                V.scalar_tensor_tensor(nw[0:R, :], yacc[0:R, :], tiny[0:R, 3:4], nw[0:R, :], ALU.mult, ALU.mult).then_inc(y_scaled, 1)

            def sheads(t, part):
                dve.wait_ge(h_in, 16 * (t + 1))
                dve.wait_ge(sconsts_in, 48)
                link(V.memset(S[0:NS, 0:1024], 0.0))
                q = Hb[0:NS, 0:512].rearrange("p (h d) -> p h d", h=HA)
                link(V.tensor_copy(qpad[:, 0:4, 0, :], q[:, 0:8:2, :]))
                V.tensor_copy(qpad[:, 4:8, 1, :], q[:, 1:8:2, :]).then_inc(qpad_ready, 1)
                link(V.tensor_copy(ptf[:], pt[:]))
                link(V.tensor_scalar(ptf[:], ptf[:], 8.0, main[:, 276:277], ALU.mult, ALU.add))
                V.tensor_copy(gi[:], ptf[:]).then_inc(gi_ready, 1)
                copied(dve, ("qrT", t))
                qf = spare[:, 512:640]
                b = filled(dve, ("decayed", t))
                release(V.tensor_tensor(S[0:NS, 1280:1408], b[0:NS, 0:128], s32[:, 0:128], ALU.mult), ("decayed", t))
                tt(qf, qf, s128[:, 0:128], ALU.mult)
                bm = s128[:, 128:384].rearrange("p (b n) -> p b n", b=NB)
                V.tensor_tensor(qdm, qrS[:, None, :, :].broadcast_to((P, NB, HR, NS)), bm[:, :, None, :].broadcast_to((P, NB, HR, NS)),
                                ALU.mult).then_inc(qd_ready, 1)
                filled(dve, ("krT", t))
                kr = Hb[0:NS, KR:KR + 512].rearrange("p (h d) -> p h d", h=HR)
                tt(kr, kr, s32[:, 128:132, None].broadcast_to((NS, HR, RD)), ALU.mult)

            def sstates(t, part):
                for k in range(NB + 1):
                    if k < NB:
                        if k >= 2:
                            filled(dve, ("sstate", k - 2))
                        V.tensor_scalar(mid[0:NS, k % 2, :], Hb[0:NS, KR:KR + 512], s32[:, 132 + k:133 + k], None, ALU.mult).then_inc(kdm_ready, 1)
                    if k:
                        b = filled(dve, ("sstate", k - 1))
                        for h in range(HR):
                            ins = V.scalar_tensor_tensor(states[:, k - 1, h, :], states[:, k - 1, h, :], float(np.exp(LOGG[h] * NT)),
                                                         b[:, h * RD:(h + 1) * RD], ALU.mult, ALU.add)
                            if h < HR - 1:
                                link(ins)
                        release(ins, ("sstate", k - 1))
                        released(dve, ("sstate", k - 1))
                        V.memset(tiny[0:1, 36:37], 0.0).then_inc(states_new, 1)
                V.memset(tiny[0:1, 38:39], 0.0).then_inc(kd_ready, 1)
                dve.wait_ge(kd_ready, t + 1)

            def sturn(t, part):
                filled(dve, ("qaT", t))
                rep = s32[:, 140:396].rearrange("p (b n) -> p b n", b=NB)
                new = S[0:NS, 1024:1280].rearrange("p (b h t) -> p b h t", b=NB, h=HA)
                link(V.tensor_tensor(new, rep.rearrange("p b (h t) -> p b h t", h=HA),
                                     Hb[0:NS, None, WI:WI + HI, None].broadcast_to((NS, NB, HA, NT)), ALU.mult))
                past = S[0:NS, 0:1024].rearrange("p (b q n) -> p b q n", b=NB, q=P // NS)
                V.tensor_copy(past, S[0:NS, 1024:1280].rearrange("p (b n) -> p b n", b=NB)[:, :, None, :].broadcast_to(
                    (NS, NB, P // NS, NS))).then_inc(wi_spread, 1)
                b = filled(dve, ("wiT", t))
                link(V.tensor_copy(wi_new, b[:, 256:320]))
                release(V.tensor_tensor(wi_past, b[:, 0:256].rearrange("p (b n) -> p b n", b=NB)[:, :, None, :].broadcast_to(
                    (P, NB, P // NS, NS)), quarter[:, None, :, None].broadcast_to((P, NB, P // NS, NS)), ALU.mult), ("wiT", t))

            def sscores(t, b_):
                if b_ < NB:
                    return
                b = filled(dve, ("snsum", t))
                release(V.tensor_copy(scs[:, PAST:SL], b[0:NS, 0:NS]), ("snsum", t))
                released(dve, ("snsum", t))
                dve.wait_ge(scores_in, 16 * (P // NS))
                past = scs[:, 0:PAST].rearrange("r (p k) -> r k p", k=BLK)
                for q in range(P // NS):
                    k = 8 * (q // 2) + q % 2
                    ins = V.tensor_copy(past[:, k:min(k + 8, BLK):2, :], S[0:NS, 512 * q:512 * (q + 1)].rearrange("r (j p) -> r j p", j=4))
                ins.then_inc(scores_placed, 1)
                dve.wait_ge(scores_placed, 1)

            def sattend(t, g):
                copied(dve, ("slog", 4 * g + 3, 4))
                for c in range(5):
                    w = 512 if c < 4 else NS
                    b = filled(dve, ("smask", g, c))
                    d = S[:, 512 * c:512 * c + w]
                    ins = V.tensor_tensor_reduce(d, d, b[:, 0:w], 1.0, -3.0e38, ALU.add, ALU.max, tiny[:, 40 + c:41 + c])
                    release(ins, ("smask", g, c))
                released(dve, ("smask", g, 4))
                link(V.tensor_reduce(tiny[:, 48:49], tiny[:, 40:45], AX.X, ALU.max))
                V.tensor_scalar(nmx[:, g:g + 1], tiny[:, 48:49], -HD ** -0.5, None, ALU.mult).then_inc(smax_ready, 1)

            def svalues(t, part):
                g = part // 2
                if part % 2 == 0:
                    return
                dve.wait_ge(sexp_ready, g + 1)
                link(V.reciprocal(tiny[:, 50:51], rs[:, g:g + 1]))
                o = filled(dve, ("satt", g))
                release(V.scalar_tensor_tensor(so[:, g, :], o[:, 0:P], tiny[:, 50:51], s128[:, 384:512], ALU.mult, ALU.mult), ("satt", g))
                released(dve, ("satt", g))
                V.memset(tiny[0:1, 36:37], 0.0).then_inc(so_ready, 1)
                if g == 1:
                    V.memset(tiny[0:1, 38:39], 0.0).then_inc(mix_ready, 1)

            steps = {"project": project, "retain": retain, "retained": retained, "scores": scores, "topk": topk,
                     "mask": mask, "attend": attend, "output": output, "norm": norm, "choose": choose, "peer": peer,
                     "finish": finish, "sheads": sheads, "sstates": sstates,
                     "sturn": sturn, "sscores": sscores, "sattend": sattend,
                     "svalues": svalues}
            for what, t, part in schedule:
                if what in steps:
                    steps[what](t, part)

        @block.scalar
        def _(act):
            A = nc.scalar

            def project(t, part):
                R = rows(t)

                def scale_turned(u):
                    Ru = rows(u)
                    for g in range(2):
                        b = filled(act, ("xT", u, g))
                        for k in range(4):
                            ins = A.activation(xT[u % 2][:, 4 * g + k, 0:Ru], b[:, k * Ru:(k + 1) * Ru], ACT.Copy, scale=colw[:, 4 * g + k:4 * g + k + 1])
                        release(ins, ("xT", u, g))

                if t == 0:
                    act.wait_ge(consts_in, 32)
                    A.activation(tinya[0:1, 0:4], main[0:1, 0:4], ACT.Copy).then_inc(act_chain, 1)
                    act.wait_ge(act_chain, 1)
                    scale_turned(0)
                if t < SAMPLE:
                    scale_turned(t + 1)
                act.wait_ge(x_scaled, t + 1)
                if t >= 2:
                    act.wait_ge(h_stored[t % 2], 64 * (t // 2))
                for n in range(7):
                    w = min(512, INW - 512 * n)
                    b = filled(act, ("proj", t, n))
                    release(A.activation(H[t % 2][0:R, 512 * n:512 * n + w], b[0:R, 0:w], ACT.Copy, scale=tiny[0:R, t % 2:t % 2 + 1]), ("proj", t, n))
                released(act, ("proj", t, 6))
                A.activation(tinya[0:1, 0:1], tinya[0:1, 1:2], ACT.Copy).then_inc(h_ready, 1)
                for u in ([t - 1] if t else []) + ([t] if t == SAMPLE else []):
                    Ru = rows(u)
                    b = filled(act, ("keysT", u))
                    if u < TILES:
                        A.activation(kT[:, u * P:(u + 1) * P], b[:, 0:P], ACT.Copy)
                        ins = A.activation(kiT[:, u * P:(u + 1) * P], b[:, 128:256], ACT.Copy)
                    else:
                        A.activation(knew[:, 0, :], b[:, 0:Ru], ACT.Copy)
                        ins = A.activation(knew[:, 1, :], b[:, 128:128 + Ru], ACT.Copy)
                    release(ins, ("keysT", u))
                    released(act, ("keysT", u))
                    A.activation(tinya[0:1, 0:1], tinya[0:1, 1:2], ACT.Copy).then_inc(keys_kept, 1)

            def turn(t, part):
                if t == 0:
                    act.wait_ge(h_in, 16)
                for name, dst in (("qiT", qiT), ("qaT", qaT)):
                    b = filled(act, (name, t))
                    src = b[:, :].rearrange("p (g n) -> p g n", g=4)
                    A.activation(dst[:, 0:8:2, :], src, ACT.Copy, scale=main[:, 277:278])
                    release(A.activation(dst[:, 1:8:2, :], src, ACT.Copy, scale=main[:, 278:279]), (name, t))
                for name, dst in (("qrT", qrT), ("krT", krT)):
                    b = filled(act, (name, t))
                    release(A.activation(dst[:].rearrange("p g n -> p (g n)"), b[:, :], ACT.Copy), (name, t))

            def retained(t, part):
                R = rows(t)
                if t < TILES:
                    filled(act, ("state", t))
                else:
                    act.wait_ge(kd_ready, t + 1)
                act.wait_ge(h_in, 16 * (t + 1))
                A.activation(Hb[0:R, KR:KR + 512], Hb[0:R, GR:GR + 512], ACT.Silu).then_inc(silu_ready, 1)

            def scores(t, c):
                w = min(512, (t + 1) * P - 512 * c)
                for h in range(HI):
                    m = score_no[(t, c, h)]
                    b = filled(act, ("score", t, c, h))
                    if m >= 2:
                        act.wait_ge(relu_used, m - 1)
                    release(A.activation(mid[:, m % 2, 0:w], b[:, 0:w], ACT.Relu), ("score", t, c, h))

            def attend(t, h):
                nch = (t + 4) // 4
                L = (t + 1) * P
                if h:
                    g = h - 1
                    for c in range(nch):
                        n = min(4, t + 1 - 4 * c)
                        m = turned_no[(t, g, c)]
                        b = filled(act, ("pT", t, g, c))
                        if m - 2 >= turned_no[(t, 0, 0)]:
                            act.wait_ge(pT_used, m - 1 - t)
                        release(A.activation(mid[:, m % 2, 0:n * P], b[:, 0:n * P], ACT.Copy), ("pT", t, g, c))
                if h < HA:
                    act.wait_ge(logits_ready, 8 * t + h + 1)
                    s_h = S[:, 1024 * (h % 2):1024 * (h % 2) + L]
                    A.activation(s_h, s_h, ACT.Exp, bias=nmx[:, h:h + 1], scale=HD ** -0.5, accum_out=rs[:, h:h + 1]).then_inc(probs_ready, 1)

            def output(t, part):
                R = rows(t)
                mixT = spare[:, 0:1024].rearrange("p (k n) -> p k n", k=KC)
                nT = spare[:, 1024:2048].rearrange("p (k n) -> p k n", k=KC)

                def keep(name, dst, g):
                    b = filled(act, (name, t, g))
                    src = b[:, 0:4 * R].rearrange("p (k n) -> p k n", k=4)
                    release(A.activation(dst[:, 4 * g:4 * g + 4, 0:R], src, ACT.Copy), (name, t, g))

                if part == 0:
                    keep("mixT", mixT, 0)
                    b = filled(act, ("mixT", t, 1))
                    for k in range(4):
                        ins = A.activation(mixT[:, 4 + k, 0:R], b[:, k * R:(k + 1) * R], ACT.Copy, scale=colw[:, 8 + k:9 + k])
                    release(ins, ("mixT", t, 1))
                elif part == 2:
                    keep("nT", nT, 0)
                    keep("nT", nT, 1)
                    keep("peerq", mixT, 0)
                elif part == 3:
                    keep("peerq", mixT, 1)
                if part < 4:
                    return
                for n in range(4 if t < TILES else 1):
                    b = filled(act, ("keys", t, n))
                    release(A.activation(Hb[:, 512 * n:512 * (n + 1)], b[:, :], ACT.Copy), ("keys", t, n))

            def choose(t, part):
                if part != 3:
                    return
                act.wait_ge(gate_shifted, t + 1)
                g = gate[:, t % 2, 0:heads_of(t)]
                A.activation(g, g, ACT.Exp).then_inc(gate_exp, 1)

            def peer(t, part):
                b0, n = part
                b0 += (SLOTS // RING) * t
                select = ident if t < TILES else fold
                W = P if t < TILES else NS
                with times(act, n) as i:
                    for j, (s0, s1) in enumerate(GROUPS):
                        n0 = len(GROUPS) * b0 + j + 1
                        act.wait_ge(hval_ready, i * len(GROUPS) + n0)
                        A.activation(gl[:, s0:s1], hv[:, s0:s1], ACT.Gelu).then_inc(gelu_ready, 1)
                        act.wait_ge(coef_ready, i * len(GROUPS) + n0)
                        for s in range(s0, s1):
                            act.wait_ge(row_used, i * RING + (RING * b0 + s + 1 + RING - 4))
                            A.activation(diag[:, s % 4, 0:W], select[:, 0:W], ACT.Copy, scale=coef[:, s:s + 1]).then_inc(diag_ready, 1)

            def sheads(t, part):
                b = filled(act, ("qiT", t))
                for a, first, pair in ((0, 0, 0), (0, 1, 5), (1, 1, 0), (1, 0, 4)):
                    src = b[:, NS * pair:NS * (pair + 4)].rearrange("p (h b t) -> p h b t", h=4, b=NB)
                    ins = A.activation(qiS[:, a, :, first:HI:2, :].rearrange("p b h t -> p h b t"), src, ACT.Copy,
                                       scale=main[:, 277 + a:278 + a])
                release(ins, ("qiT", t))
                for name, dst in (("qrT", spare[:, 512:640]), ("krT", spare[:, 640:768])):
                    b = filled(act, (name, t))
                    release(A.activation(dst, b[:, 0:128], ACT.Copy), (name, t))

            def sturn(t, part):
                b = filled(act, ("qaT", t))
                release(A.activation(qaS.rearrange("p b h t -> p h b t"), b[:, 0:256].rearrange("p (h b t) -> p h b t", h=HI, b=NB), ACT.Copy), ("qaT", t))

            def sscores(t, b_):
                if b_ < NB:
                    for half in range(2):
                        b = filled(act, ("skT", b_, half))
                        release(A.activation(mid[:, half, :], b[:, :], ACT.Copy), ("skT", b_, half))
                    b = filled(act, ("sdot", b_))
                    release(A.activation(positive[b_ % 2], b[:, :], ACT.Relu), ("sdot", b_))
                    return
                b = filled(act, ("ssum", t))
                release(A.activation(mid[:, 0, :], b[:, :], ACT.Copy), ("ssum", t))
                b = filled(act, ("snew", t))
                release(A.activation(positive[2], b[:, 0:2 * NS], ACT.Relu), ("snew", t))

            def slogits(t, b_):
                if b_ == 0:
                    act.wait_ge(scores_placed, 1)
                for c in range(6):
                    if c < 4:
                        b = filled(act, ("sKT", b_, c))
                        release(A.activation(mid[:, c % 2, :], b[:, :], ACT.Copy), ("sKT", b_, c))
                    if c:
                        w = 512 if c < 5 else NS
                        p0 = 32 * (b_ % 4)
                        b = filled(act, ("slog", b_, c - 1))
                        release(A.activation(S[p0:p0 + 32, 512 * (c - 1):512 * (c - 1) + w], b[p0:p0 + 32, 0:w], ACT.Copy), ("slog", b_, c - 1))

            def sattend(t, g):
                pTs = Hb[:, 768:2816].rearrange("p (k n) -> p k n", k=BLK)
                act.wait_ge(smax_ready, g + 1)
                A.activation(S[:, 0:SL], S[:, 0:SL], ACT.Exp, bias=nmx[:, g:g + 1], scale=HD ** -0.5, accum_out=rs[:, g:g + 1]).then_inc(sexp_ready, 1)
                for c in range(5):
                    b = filled(act, ("spT", g, c))
                    if c < 4:
                        ins = A.activation(pTs[:, 4 * c:4 * c + 4, :], b[:, :].rearrange("p (k n) -> p k n", k=4), ACT.Copy)
                    else:
                        ins = A.activation(knewp, b[0:NS, 0:P], ACT.Copy)
                    release(ins, ("spT", g, c))

            steps = {"project": project, "turn": turn, "retained": retained, "scores": scores, "attend": attend,
                     "output": output, "choose": choose, "peer": peer, "sheads": sheads, "sturn": sturn, "sscores": sscores,
                     "slogits": slogits, "sattend": sattend}
            for what, t, part in schedule:
                if what in steps:
                    steps[what](t, part)

        @block.gpsimd
        def _(pool):
            table_ik = cache_ik.rearrange("(r k) d -> r (k d)", k=BLK)
            table_k = cache_k.rearrange("(r k) d -> r (k d)", k=BLK)
            table_v = cache_v.rearrange("(r k) d -> r (k d)", k=BLK)

            def gather(dst, table, ids, s):
                pool.indirect_dma_start(dst, None, table, bass.IndirectOffsetOnAxis(ap=ids, axis=0)).then_inc(s, 16)

            def peer(t, b, n):
                ids = eid[:].rearrange("p a n -> p (a n)")
                b0 = (SLOTS // RING) * t + b

                def gather_block(i, k):
                    now = idx8[:, (b + k) % 2, :]
                    nc.gpsimd.tensor_copy(now, ids[:, bass.ds(i * 2 * RING + ((t % 2) * SLOTS + RING * (b + k)), RING)]).then_inc(idx_ready, 1)
                    pool.wait_ge(idx_ready, i * 2 + (b0 + k + 1))
                    for s in range(RING):
                        pool.wait_ge(row_used, i * 2 * RING + (RING * (b0 + k) + s + 1))
                        pool.sem_inc(slot_granted, 1)
                        gather(ring[:, s, :], uv, now[:, s:s + 1], row_in[s])

                pool.wait_ge(chosen, t + 1)
                if n >= 2:
                    with times(pool, n // 2) as i:
                        gather_block(i, 0)
                        gather_block(i, 1)
                if n % 2:
                    gather_block(0, n - 1)

            runs = []
            for what, t, part in schedule:
                b, n = part if what == "peer" else (part, 1)
                if what == "peer" and runs and runs[-1][0:2] == ["peer", t]:
                    runs[-1][3] += n
                elif what in ("peer", "sscores", "slogits", "sattend", "svalues") and (what, part) != ("sscores", NB):
                    runs.append([what, t, b, n])
            for what, t, part, count in runs:
                if what == "peer":
                    if t == 0 and part == 0:
                        pool.wait_ge(rotated, TILES + 1)
                        pool.wait_ge(h_ready, TILES + 1)
                    peer(t, part, count)
                elif what == "sscores":
                    if part == 0:
                        pool.wait_ge(gi_ready, 1)
                        pool.wait_ge(states_out, 16)
                    if part >= 2:
                        filled(pool, ("skT", part - 2, 1))
                    gather(G[:, 1024 * (part % 2):1024 * (part % 2 + 1)], table_ik, gi[:, part:part + 1], g_in[part % 2])
                elif what == "slogits":
                    if part == 0:
                        filled(pool, ("skT", NB - 1, 1))
                    elif part in (4, 5):
                        pool.wait_ge(g_used, part - 1)
                    elif part % 4 >= 2:
                        filled(pool, ("sKT", part - 2, 3))
                    gather(gathered[part % 2], table_k, gi[:, part:part + 1], g_in[part % 2])
                elif what in ("sattend", "svalues"):
                    g, batches = (part, (0,)) if what == "sattend" else (part // 2, (3,) if part % 2 else (1, 2))
                    for bb in batches:
                        if bb == 0:
                            filled(pool, ("sKT", 4 * g + 2, 3))
                        elif bb == 1:
                            filled(pool, ("spT", g, 4))
                        else:
                            pool.wait_ge(g_used, 4 * g + bb - 1)
                        gather(gathered_v[bb % 2], table_v, gi[:, 4 * g + bb:4 * g + bb + 1], g_in[bb % 2])


_NAMES = ["x_p", "x_s", "cache_k", "cache_v", "cache_ik", "state_in", "pages", "w_in", "w_out", "w_q", "sk", "uv",
          "cols", "wffn", "wfin", "c_rope", "c_main", "c_dec", "c_s32", "c_s128", "c_fold"]
_OUTS = [("y_p", (SEQ, D)), ("y_s", (NS, D)), ("k_p", (SEQ, 128)), ("v_p", (SEQ, 128)), ("ik_p", (SEQ, 64)),
         ("st_p", (P, HR * RD)), ("k_s", (NS, 128)), ("v_s", (NS, 128)), ("ik_s", (NS, 64)), ("st_s", (P, NB, HR, RD))]


def kernel(x_prompt, x_sample, cache_k, cache_v, cache_idx_k, state_ret, page_table,
           norm_attn_w, w_in, ret_gn_w, w_out, norm_ffn_w, peer_w_q,
           peer_sub_keys_1, peer_sub_keys_2, peer_u, peer_v, final_norm_w):
    import numpy as _np
    import concourse.bacc as _bacc
    from concourse import mybir as _mybir
    from concourse.bass_utils import run_bass_kernel_spmd as _run

    a = _np.asarray
    heads = _np.arange(HA * HD).reshape(KVH, HA // KVH, HD).transpose(1, 0, 2).ravel()
    order_in = _np.concatenate([heads, _np.arange(512, INW)])
    order_out = _np.concatenate([heads, _np.arange(512, D)])
    rope, main, dec, s32, s128, fold = constants()
    sk = _np.zeros((P, 256), _np.float32)
    sk[0:64, 0:128] = a(peer_sub_keys_1)[0].T
    sk[64:128, 128:256] = a(peer_sub_keys_2)[0].T
    arrays = {
        "x_p": a(x_prompt)[0], "x_s": a(x_sample).reshape(NS, D),
        "cache_k": a(cache_k).reshape(-1, 128), "cache_v": a(cache_v).reshape(-1, 128),
        "cache_ik": a(cache_idx_k).reshape(-1, 64),
        "state_in": a(state_ret)[0].transpose(2, 0, 1, 3),
        "pages": _np.repeat(a(page_table).T, 8, axis=0),
        "w_in": a(w_in)[0][:, order_in], "w_out": a(w_out)[0][order_out], "w_q": a(peer_w_q)[0], "sk": sk,
        "uv": _np.concatenate([a(peer_u)[0], a(peer_v)[0]], axis=1),
        "cols": _np.concatenate([a(norm_attn_w).reshape(8, P).T, a(ret_gn_w).reshape(4, P).T], axis=1),
        "wffn": a(norm_ffn_w)[0], "wfin": a(final_norm_w),
        "c_rope": rope, "c_main": main, "c_dec": dec, "c_s32": s32, "c_s128": s128, "c_fold": fold,
    }
    nc = _bacc.Bacc("TRN2", target_bir_lowering=False, num_devices=1)
    feed, args = {}, []
    for name in _NAMES:
        v = _np.ascontiguousarray(arrays[name])
        feed[f"in_{name}"] = v
        args.append(nc.dram_tensor(f"in_{name}", v.shape, _mybir.dt.from_np(v.dtype), kind="ExternalInput").ap())
    for name, shape in _OUTS:
        args.append(nc.dram_tensor(f"out_{name}", shape, F32, kind="ExternalOutput").ap())
    build(nc, *args)
    r = _run(nc, [feed], core_ids=[0]).results[0]
    y_p, y_s, k_p, v_p, ik_p, st_p, k_s, v_s, ik_s, st_s = (a(r[f"out_{n}"]) for n, _ in _OUTS)
    return (y_p.reshape(1, SEQ, D), y_s.reshape(NB, NT, D),
            k_p.reshape(1, 1, SEQ, KVH, HD), v_p.reshape(1, 1, SEQ, KVH, HD), ik_p.reshape(1, 1, SEQ, HD),
            st_p.reshape(P, HR, RD).transpose(1, 0, 2)[None, None],
            k_s.reshape(1, NB, NT, KVH, HD), v_s.reshape(1, NB, NT, KVH, HD), ik_s.reshape(1, NB, NT, HD),
            st_s.transpose(1, 2, 0, 3)[None])
```
